# Optimizing a Trainium2 kernel written in Bass

```python
import jax, jax.numpy as jnp
from jax import lax
import numpy as np

D_MODEL = 1024
BATCH = 1
SEQ = 128
DEPTH = 1
DEC_BATCH = 1
DEC_SEQ = 1024
PAST_LEN = 128

F32 = jnp.float32
GRID_W = 64
EPS = 1e-6
NEG = -1e30
M_HEADS = 4
M_WIDTH = D_MODEL // 2
M_DH = M_WIDTH // M_HEADS
M_CHUNK = 64
A_HEADS = 8
A_KV = 2
A_REP = A_HEADS // A_KV
A_DH = (D_MODEL // 2) // A_HEADS
WINDOW = 128
BLOCK = 128
ROPE_BASE = 10000.0
IN_SIZES = (M_WIDTH, M_WIDTH, M_WIDTH, M_WIDTH, 4 * M_HEADS, A_HEADS * A_DH, A_KV * A_DH, A_KV * A_DH)
IN_COLS = 4 * M_WIDTH + 4 * M_HEADS + (A_HEADS + 2 * A_KV) * A_DH
N_KEYS = 128
N_EXPERTS = N_KEYS * N_KEYS
P_HEADS = 8
P_DKEY = 256
P_HALF = P_DKEY // 2
P_TOPK = 16
P_TOKBLK = 128

kernel_name = 'hybrid_mlstm_swa_peer_diffusion_step'

def rmsnorm(x, g):
    xf = x.astype(F32)
    y = xf * lax.rsqrt(jnp.mean(xf * xf, axis=-1, keepdims=True) + EPS)
    return (y * g.astype(F32)).astype(x.dtype)

def modulate(h, shift, scale):
    return h * (1 + scale[:, None, :]) + shift[:, None, :]

def split_cols(z):
    outs, off = [], 0
    for s in IN_SIZES:
        outs.append(z[..., off:off + s])
        off += s
    return outs

def rope_2d(x):
    T = x.shape[1]
    rows = T // GRID_W
    row = jnp.repeat(jnp.arange(rows, dtype=F32), GRID_W)
    col = jnp.tile(jnp.arange(GRID_W, dtype=F32), rows)
    half = A_DH // 2
    quarter = half // 2
    inv = ROPE_BASE ** (-jnp.arange(quarter, dtype=F32) / quarter)
    xf = x.astype(F32)

    def rot(xa, pos):
        ang = pos[:, None] * inv[None, :]
        cos = jnp.cos(ang)[None, :, None, :]
        sin = jnp.sin(ang)[None, :, None, :]
        x1, x2 = xa[..., :quarter], xa[..., quarter:]
        return jnp.concatenate([x1 * cos - x2 * sin, x1 * sin + x2 * cos], axis=-1)

    return jnp.concatenate([rot(xf[..., :half], row), rot(xf[..., half:], col)], axis=-1).astype(x.dtype)

def mlstm_chunkwise(q, k, v, li, lf, C0, n0, m0):
    B, T, H, dh = q.shape
    nc = T // M_CHUNK

    def chunks(a):
        return jnp.moveaxis(a.reshape((B, nc, M_CHUNK) + a.shape[2:]), 1, 0)

    lower = jnp.tril(jnp.ones((M_CHUNK, M_CHUNK), dtype=bool))

    def step(carry, inp):
        C, n, m = carry
        qc, kc, vc, lic, lfc = inp
        b = jnp.swapaxes(jnp.cumsum(lfc, axis=1), 1, 2)
        ig = jnp.swapaxes(lic, 1, 2)
        a_inter = b + m[..., None]
        d = jnp.where(lower, b[..., :, None] - b[..., None, :] + ig[..., None, :], -jnp.inf)
        m_t = jnp.maximum(a_inter, jnp.max(d, axis=-1))
        w_inter = jnp.exp(a_inter - m_t)
        s = jnp.einsum('blhd,bshd->bhls', qc, kc) * jnp.exp(d - m_t[..., None])
        num = (jnp.einsum('bhls,bshv->blhv', s, vc)
               + jnp.swapaxes(w_inter, 1, 2)[..., None] * jnp.einsum('blhk,bhkv->blhv', qc, C))
        den = jnp.sum(s, axis=-1) + w_inter * jnp.einsum('blhk,bhk->bhl', qc, n)
        den = jnp.maximum(jnp.abs(den), jnp.exp(-m_t))
        h = num / jnp.swapaxes(den, 1, 2)[..., None]
        m_new = m_t[..., -1]
        g = jnp.exp(b[..., -1:] - b + ig - m_new[..., None])
        decay = jnp.exp(b[..., -1] + m - m_new)
        C_new = decay[..., None, None] * C + jnp.einsum('bhs,bshk,bshv->bhkv', g, kc, vc)
        n_new = decay[..., None] * n + jnp.einsum('bhs,bshk->bhk', g, kc)
        return (C_new, n_new, m_new), h

    (C, n, m), hs = lax.scan(step, (C0, n0, m0), tuple(chunks(a) for a in (q, k, v, li, lf)))
    return jnp.moveaxis(hs, 0, 1).reshape(B, T, H, dh), (C, n, m)

def mlstm_mixer(mq, mk, mv, mo, gt, b_gates, mh_g, st_f, st_b):
    B, T, _ = mq.shape

    def heads(a):
        return a.astype(F32).reshape(B, T, M_HEADS, M_DH)

    q = heads(mq) * (M_DH ** -0.5)
    k = heads(mk)
    v = heads(mv)
    g = (gt.astype(F32) + b_gates.astype(F32)).reshape(B, T, 4, M_HEADS)
    li_f, lf_f = g[:, :, 0], jax.nn.log_sigmoid(g[:, :, 1])
    li_b, lf_b = g[:, :, 2], jax.nn.log_sigmoid(g[:, :, 3])
    h_f, fin_f = mlstm_chunkwise(q, k, v, li_f, lf_f, *st_f)

    def rev(a):
        return jnp.flip(a, axis=1)

    h_b, fin_b = mlstm_chunkwise(rev(q), rev(k), rev(v), rev(li_b), rev(lf_b), *st_b)
    h = h_f + rev(h_b)
    h = h * lax.rsqrt(jnp.mean(h * h, axis=-1, keepdims=True) + EPS) * mh_g.astype(F32).reshape(M_HEADS, M_DH)
    out = jax.nn.sigmoid(mo.astype(F32)) * h.reshape(B, T, M_WIDTH)
    return out.astype(mq.dtype), fin_f, fin_b

def sink_attend(s, sink, vals):
    sk = sink.astype(F32).reshape(1, A_KV, A_REP, 1, 1)
    mx = jnp.maximum(jnp.max(s, axis=-1, keepdims=True), sk)
    p = jnp.exp(s - mx)
    den = jnp.sum(p, axis=-1, keepdims=True) + jnp.exp(sk - mx)
    return jnp.einsum('bgrqk,bkgd->bqgrd', p / den, vals.astype(F32))

def attn_context(q, k, v, sink):
    B, S = q.shape[:2]
    nb = S // BLOCK
    scale = A_DH ** -0.5
    qb = jnp.moveaxis(q.astype(F32).reshape(B, nb, BLOCK, A_KV, A_REP, A_DH), 1, 0)
    kf = k.astype(F32)

    def one(qblk):
        s = jnp.einsum('bqgrd,bkgd->bgrqk', qblk, kf) * scale
        return sink_attend(s, sink, v)

    out = lax.map(one, qb)
    return jnp.moveaxis(out, 0, 1).reshape(B, S, A_HEADS * A_DH)

def attn_latent(q, k, v, kc, vc, sink):
    B, T = q.shape[:2]
    nb = T // BLOCK
    scale = A_DH ** -0.5
    qb = jnp.moveaxis(q.astype(F32).reshape(B, nb, BLOCK, A_KV, A_REP, A_DH), 1, 0)
    pad = ((0, 0), (BLOCK, BLOCK), (0, 0), (0, 0))

    def windows(a):
        ap = jnp.pad(a.astype(F32), pad).reshape(B, nb + 2, BLOCK, A_KV, A_DH)
        w = jnp.concatenate([ap[:, :-2], ap[:, 1:-1], ap[:, 2:]], axis=2)
        return jnp.moveaxis(w, 1, 0)

    kw, vw = windows(k), windows(v)
    qpos = jnp.arange(nb)[:, None] * BLOCK + jnp.arange(BLOCK)[None, :]
    kpos = jnp.arange(nb)[:, None] * BLOCK - BLOCK + jnp.arange(3 * BLOCK)[None, :]
    mask = ((kpos[:, None, :] >= 0) & (kpos[:, None, :] < T)
            & (jnp.abs(kpos[:, None, :] - qpos[:, :, None]) <= WINDOW))
    kcf, vcf = kc.astype(F32), vc.astype(F32)

    def one(args):
        qblk, kblk, vblk, mblk = args
        s_c = jnp.einsum('bqgrd,bkgd->bgrqk', qblk, kcf) * scale
        s_w = jnp.where(mblk, jnp.einsum('bqgrd,bkgd->bgrqk', qblk, kblk) * scale, NEG)
        s = jnp.concatenate([s_c, s_w], axis=-1)
        vals = jnp.concatenate([vcf, vblk], axis=1)
        return sink_attend(s, sink, vals)

    out = lax.map(one, (qb, kw, vw, mask))
    return jnp.moveaxis(out, 0, 1).reshape(B, T, A_HEADS * A_DH)

def peer(h, w_q, sub_a, sub_b, u_tab, v_tab):
    B, T, D = h.shape
    N = B * T
    x = h.reshape(N, D)
    q = (x @ w_q).astype(F32).reshape(N, P_HEADS, P_DKEY)
    sa = jnp.einsum('nhd,kd->nhk', q[..., :P_HALF], sub_a.astype(F32))
    sb = jnp.einsum('nhd,kd->nhk', q[..., P_HALF:], sub_b.astype(F32))
    va, ia = lax.top_k(sa, P_TOPK)
    vb, ib = lax.top_k(sb, P_TOPK)
    cand = (va[..., :, None] + vb[..., None, :]).reshape(N, P_HEADS, P_TOPK * P_TOPK)
    cidx = (ia[..., :, None] * N_KEYS + ib[..., None, :]).reshape(N, P_HEADS, P_TOPK * P_TOPK)
    top, pos = lax.top_k(cand, P_TOPK)
    eidx = jnp.take_along_axis(cidx, pos, axis=-1)
    gates = jax.nn.softmax(top, axis=-1).astype(h.dtype)
    nblk = N // P_TOKBLK

    def blk(args):
        xb, eb, gb = args
        a = jax.nn.gelu(jnp.einsum('pd,phkd->phk', xb, u_tab[eb]))
        return jnp.einsum('phk,phkd->pd', gb * a, v_tab[eb])

    out = lax.map(blk, (x.reshape(nblk, P_TOKBLK, D),
                        eidx.reshape(nblk, P_TOKBLK, P_HEADS, P_TOPK),
                        gates.reshape(nblk, P_TOKBLK, P_HEADS, P_TOPK)))
    return out.reshape(B, T, D).astype(h.dtype)

def trunk_layer(x, cvec, prm, ctx_cache):
    (w_ada, b_ada, n1, n2, w_in, b_g, mh_g, qg, kg, sink, w_out, pwq, psa, psb, pu, pv) = prm
    B, T, _ = x.shape
    sh1, sc1, g1, sh2, sc2, g2 = jnp.split(jax.nn.silu(cvec) @ w_ada + b_ada, 6, axis=-1)
    h = modulate(rmsnorm(x, n1), sh1, sc1)
    mq, mk, mv, mo, gt, aq, ak, av = split_cols(h @ w_in)
    q = rmsnorm(aq.reshape(B, T, A_HEADS, A_DH), qg)
    k = rmsnorm(ak.reshape(B, T, A_KV, A_DH), kg)
    v = av.reshape(B, T, A_KV, A_DH)
    if ctx_cache is None:
        zero = (jnp.zeros((B, M_HEADS, M_DH, M_DH), F32), jnp.zeros((B, M_HEADS, M_DH), F32),
                jnp.full((B, M_HEADS), NEG, F32))
        m_out, fin_f, fin_b = mlstm_mixer(mq, mk, mv, mo, gt, b_g, mh_g, zero, zero)
        a_out = attn_context(q, k, v, sink)
        new = (k, v, jnp.stack([fin_f[0], fin_b[0]], axis=1), jnp.stack([fin_f[1], fin_b[1]], axis=1),
               jnp.stack([fin_f[2], fin_b[2]], axis=1))
    else:
        kc, vc, C0, n0, m0 = ctx_cache
        C0, n0, m0 = C0.astype(F32), n0.astype(F32), m0.astype(F32)
        m_out, _, _ = mlstm_mixer(mq, mk, mv, mo, gt, b_g, mh_g,
                                  (C0[:, 0], n0[:, 0], m0[:, 0]), (C0[:, 1], n0[:, 1], m0[:, 1]))
        a_out = attn_latent(rope_2d(q), rope_2d(k), v, kc, vc, sink)
        new = None
    mix = jnp.concatenate([m_out, a_out.astype(x.dtype)], axis=-1) @ w_out
    x = x + g1[:, None, :] * mix
    h2 = modulate(rmsnorm(x, n2), sh2, sc2)
    x = x + g2[:, None, :] * peer(h2, pwq, psa, psb, pu, pv)
    return x, new

def setup_inputs(seed: int = 0) -> dict:
    key = jax.random.key(seed)
    ks = jax.random.split(key, 28)

    def nrm(k, shape, s=1.0):
        return (s * jax.random.normal(k, shape)).astype(F32)

    gate_base = jnp.tile(jnp.repeat(jnp.array([0.0, 3.0], F32), M_HEADS), 2)
    return {
        'x_prompt': nrm(ks[0], (BATCH, SEQ, D_MODEL)),
        'x_sample': nrm(ks[1], (DEC_BATCH, DEC_SEQ, D_MODEL)),
        'c': nrm(ks[2], (DEC_BATCH, D_MODEL)),
        'cache_attn_k': nrm(ks[3], (DEC_BATCH, DEPTH, PAST_LEN, A_KV, A_DH)),
        'cache_attn_v': nrm(ks[4], (DEC_BATCH, DEPTH, PAST_LEN, A_KV, A_DH)),
        'state_mlstm_C': nrm(ks[5], (DEC_BATCH, DEPTH, 2, M_HEADS, M_DH, M_DH)),
        'state_mlstm_n': nrm(ks[6], (DEC_BATCH, DEPTH, 2, M_HEADS, M_DH)),
        'state_mlstm_m': nrm(ks[7], (DEC_BATCH, DEPTH, 2, M_HEADS)),
        'c_ctx': nrm(ks[8], (D_MODEL,)),
        'w_ada': nrm(ks[9], (DEPTH, D_MODEL, 6 * D_MODEL), D_MODEL ** -0.5),
        'b_ada': nrm(ks[10], (DEPTH, 6 * D_MODEL), 0.01),
        'norm1_g': 1.0 + nrm(ks[11], (DEPTH, D_MODEL), 0.05),
        'norm2_g': 1.0 + nrm(ks[12], (DEPTH, D_MODEL), 0.05),
        'w_in': nrm(ks[13], (DEPTH, D_MODEL, IN_COLS), D_MODEL ** -0.5),
        'b_gates': gate_base + nrm(ks[14], (DEPTH, 4 * M_HEADS), 0.5),
        'mh_norm_g': 1.0 + nrm(ks[15], (DEPTH, M_WIDTH), 0.05),
        'q_norm_g': 1.0 + nrm(ks[16], (DEPTH, A_DH), 0.05),
        'k_norm_g': 1.0 + nrm(ks[17], (DEPTH, A_DH), 0.05),
        'sink_logits': nrm(ks[18], (DEPTH, A_HEADS)),
        'w_out': nrm(ks[19], (DEPTH, D_MODEL, D_MODEL), D_MODEL ** -0.5),
        'peer_w_q': nrm(ks[20], (DEPTH, D_MODEL, P_HEADS * P_DKEY), D_MODEL ** -0.5),
        'peer_sub_a': nrm(ks[21], (DEPTH, N_KEYS, P_HALF), P_HALF ** -0.5),
        'peer_sub_b': nrm(ks[22], (DEPTH, N_KEYS, P_HALF), P_HALF ** -0.5),
        'peer_u': nrm(ks[23], (DEPTH, N_EXPERTS, D_MODEL), D_MODEL ** -0.5),
        'peer_v': nrm(ks[24], (DEPTH, N_EXPERTS, D_MODEL), P_HEADS ** -0.5),
    }

def reference(x_prompt, x_sample, c, cache_attn_k, cache_attn_v, state_mlstm_C, state_mlstm_n,
              state_mlstm_m, c_ctx, w_ada, b_ada, norm1_g, norm2_g, w_in, b_gates, mh_norm_g,
              q_norm_g, k_norm_g, sink_logits, w_out, peer_w_q, peer_sub_a, peer_sub_b, peer_u, peer_v):
    def layer_params(l):
        return (w_ada[l], b_ada[l], norm1_g[l], norm2_g[l], w_in[l], b_gates[l], mh_norm_g[l],
                q_norm_g[l], k_norm_g[l], sink_logits[l], w_out[l], peer_w_q[l], peer_sub_a[l],
                peer_sub_b[l], peer_u[l], peer_v[l])

    xp = x_prompt
    cp = jnp.broadcast_to(c_ctx, (xp.shape[0], D_MODEL))
    ks_, vs_, Cs, ns, ms = [], [], [], [], []
    for l in range(DEPTH):
        xp, (k_l, v_l, C_l, n_l, m_l) = trunk_layer(xp, cp, layer_params(l), None)
        ks_.append(k_l)
        vs_.append(v_l)
        Cs.append(C_l)
        ns.append(n_l)
        ms.append(m_l)

    xs = x_sample
    for l in range(DEPTH):
        xs, _ = trunk_layer(xs, c, layer_params(l),
                            (cache_attn_k[:, l], cache_attn_v[:, l], state_mlstm_C[:, l],
                             state_mlstm_n[:, l], state_mlstm_m[:, l]))

    return (xp, xs, jnp.stack(ks_, axis=1), jnp.stack(vs_, axis=1), jnp.stack(Cs, axis=1),
            jnp.stack(ns, axis=1), jnp.stack(ms, axis=1))


_drawn_inputs = setup_inputs


def setup_inputs(seed=0):
    import zlib

    import numpy as np

    out = dict(_drawn_inputs(seed))
    spreads = {}
    factors = {'state_mlstm_C': 5.638,
     'state_mlstm_n': 8.0,
     'state_mlstm_m': 8.0,
     'mh_norm_g': 3.198,
     'q_norm_g': 7.988,
     'sink_logits': 44.354}
    for name, (base, spread) in spreads.items():
        noise = np.random.default_rng([zlib.crc32(name.encode()), seed]).standard_normal(out[name].shape)
        drawn = base * np.exp(spread * noise) if base else spread * noise
        out[name] = __import__('jax').numpy.asarray(drawn.astype(out[name].dtype))
    for name, factor in factors.items():
        out[name] = (out[name] * factor).astype(out[name].dtype)
    return out
```

```python
from contextlib import ExitStack
from itertools import chain, repeat

import numpy as np

import concourse.bass as bass
from concourse import mybir

ALU = mybir.AluOpType
ACT = mybir.ActivationFunctionType
AX = mybir.AxisListType
F32 = mybir.dt.float32
U32 = mybir.dt.uint32

P = 128
D = 1024
KD = D // P
TILES = 9
COND = 2
MH, MW = 4, 512
AH, AKV, ADH = 8, 2, 64
QKH = AH + AKV
PH, TOPK = 8, 16
SLOTS = PH * TOPK
GROUP = 8
NSIDE = 2 * PH
ADA = 6 * D
IN_COLS = 4 * MW + QKH * ADH + AKV * ADH + 4 * MH
C_Q, C_K, C_V, C_O, C_A, C_R = (i * 512 for i in range(6))
REST = IN_COLS - C_R
EPS = 1e-6
NEG = -1e30
C1 = P + 1


class Names:
    pass


class Count:

    def __init__(self, eng, sem, per=0, t=0, tick=None):
        self.eng, self.sem, self.base, self.k, self.tick = eng, sem, t * per, 0, tick

    def link(self, ins):
        self.k += 1
        ins.then_inc(self.sem, 1)
        self.eng.wait_ge(self.sem, self.base + self.k)
        if self.tick is not None:
            self.eng.sem_inc(self.tick, 1)


def conditioning(nc, g, io):
    CH = 512
    NCH = ADA // CH
    RING = 3
    with ExitStack() as ctx:
        def sb(name, shape, dt=F32):
            return ctx.enter_context(nc.sbuf_tensor(name, shape, dt))

        def sem(name):
            return ctx.enter_context(nc.semaphore(name))

        wbuf = [sb(f"ada_w{j}", [P, KD, CH]) for j in range(RING)]
        mod = sb("ada_rows", [COND, ADA])
        cond = sb("ada_cond", [P, KD, COND])
        silu = sb("ada_silu", [P, KD, COND])
        norms = sb("ada_norms", [P, 2, KD])
        sel2 = sb("ada_sel2", [COND, COND, P])
        xt = sb("ada_x", [P, 2, D])
        sq = sb("ada_sq", [P, D])
        ss = sb("ada_ss", [P, TILES])
        acc = [ctx.enter_context(nc.psum_tensor(f"ada_acc{j}", [P, CH], F32)) for j in range(RING)]
        colT = ctx.enter_context(nc.psum_tensor("ada_colT", [P, 4, KD, COND], F32))
        rowB = [ctx.enter_context(nc.psum_tensor(f"ada_rowB{j}", [P, CH], F32)) for j in range(2)]

        s_small = sem("ada_small_in")
        s_x = [sem(f"ada_x_in{j}") for j in range(2)]
        s_w = [sem(f"ada_w_in{j}") for j in range(RING)]
        s_mm = sem("ada_mm_done")
        s_free = [sem(f"ada_acc_free{j}") for j in range(RING)]
        s_exp = sem("ada_exp_done")
        s_silu = sem("ada_silu_done")
        s_sq = sem("ada_square_done")
        s_ms = sem("ada_meansq_done")
        s_rt = sem("ada_sqrt_done")
        s_dve = sem("ada_dve_chain")
        s_pool = sem("ada_pool_chain")
        s_const = sem("ada_const_done")
        s_col = sem("ada_cols_done")
        s_row = sem("ada_row_done")
        s_rowe = sem("ada_row_out")

        w_ada = io.w_ada.rearrange("(k p) n -> p k n", p=P)
        with nc.Block() as block:
            @block.sync
            def _(sp):
                sp.dma_start(cond[:], io.cond_cols).then_inc(s_small, 16)
                sp.dma_start(mod[:], io.b_ada).then_inc(s_small, 16)
                sp.dma_start(norms[:], io.norm_cols).then_inc(s_small, 16)
                for j in range(RING):
                    sp.dma_start(wbuf[j][:], w_ada[:, :, j * CH:(j + 1) * CH]).then_inc(s_w[j], 16)
                with sp.Fori(1, NCH // RING) as r:
                    for j in range(RING):
                        sp.wait_ge(s_mm, r * RING + (j + 1 - RING))
                        sp.dma_start(wbuf[j][:], w_ada[:, :, bass.ds(r * (RING * CH) + j * CH, CH)]).then_inc(s_w[j], 16)
                for k in range(KD):
                    sp.dma_start(g.w_in[:, k, :], io.w_in[k * P:(k + 1) * P, :]).then_inc(g.s_w_in, 16)

            @block.scalar
            def _(act):
                for i in range(2):
                    act.dma_start(xt[:, i, :], io.x[i]).then_inc(s_x[i], 16)
                act.wait_ge(s_small, 48)
                act.activation(silu[:], cond[:], ACT.Exp, scale=-1.0).then_inc(s_exp, 1)
                for i in range(TILES):
                    act.wait_ge(s_x[i % 2], 16 * (i // 2 + 1))
                    act.activation(sq[:], xt[:, i % 2, :], ACT.Square, accum_out=ss[:, i:i + 1]).then_inc(s_sq, 1)
                    act.wait_ge(s_sq, i + 1)
                    if i + 2 < TILES:
                        act.dma_start(xt[:, i % 2, :], io.x[i + 2]).then_inc(s_x[i % 2], 16)
                act.wait_ge(s_ms, 1)
                act.activation(g.rstd[:], g.rstd[:], ACT.Sqrt).then_inc(s_rt, 1)

            @block.gpsimd
            def _(pool):
                c = Count(pool, s_pool)
                c.link(pool.memset(g.ident[:], 0.0))
                c.link(pool.memset(g.sel[:], 0.0))
                c.link(pool.memset(sel2[:], 0.0))
                c.link(pool.memset(g.neg_after[:], 0.0))
                c.link(pool.memset(g.neg_before[:], 0.0))
                c.link(pool.affine_select(out=g.ident[:], in_=g.ident[:], compare_op=ALU.not_equal, fill=1.0,
                                          base=0, pattern=[[-1, P]], channel_multiplier=1))
                c.link(pool.affine_select(out=g.sel[:], in_=g.sel[:], compare_op=ALU.not_equal, fill=1.0,
                                          base=0, pattern=[[-1, MH], [0, P]], channel_multiplier=1))
                c.link(pool.affine_select(out=sel2[:], in_=sel2[:], compare_op=ALU.not_equal, fill=1.0,
                                          base=0, pattern=[[-1, COND], [0, P]], channel_multiplier=1))
                c.link(pool.affine_select(out=g.neg_after[:], in_=g.neg_after[:], compare_op=ALU.is_ge, fill=NEG,
                                          base=0, pattern=[[0, MH], [1, P]], channel_multiplier=-1))
                pool.affine_select(out=g.neg_before[:], in_=g.neg_before[:], compare_op=ALU.is_ge, fill=NEG,
                                   base=0, pattern=[[0, MH], [-1, P]], channel_multiplier=1).then_inc(s_const, 1)

            @block.tensor
            def _(pe):
                pe.wait_ge(s_silu, 1)
                with pe.Fori(0, NCH // RING) as r:
                    for j in range(RING):
                        pe.wait_ge(s_w[j], r * 16 + 16)
                        pe.wait_ge(s_free[j], r + 1)
                        for k in range(KD):
                            mm = pe.matmul(acc[j][0:COND, :], silu[:, k, :], wbuf[j][:, k, :],
                                           start=(k == 0), stop=(k == KD - 1))
                        mm.then_inc(s_mm, 1)
                pe.wait_ge(s_const, 1)
                for j in range(RING):
                    pe.wait_ge(s_free[j], NCH // RING + 1)
                for i, part in enumerate((0, 1, 3, 4)):
                    for k in range(KD):
                        mm = pe.transpose(colT[:, i, k, :], mod[:, part * D + k * P:part * D + (k + 1) * P],
                                          g.ident[0:COND, 0:COND])
                mm.then_inc(s_col, 1)
                n = 0
                for part in (2, 5):
                    for cnd in range(COND):
                        for half in range(2):
                            if n >= 2:
                                pe.wait_ge(s_rowe, n - 1)
                            o = part * D + half * CH
                            pe.matmul(rowB[n % 2][:], sel2[:, cnd, :], mod[:, o:o + CH],
                                      start=True, stop=True).then_inc(s_row, 1)
                            n += 1

            @block.vector
            def _(dve):
                c = Count(dve, s_dve)
                dve.wait_ge(s_exp, 1)
                dve.wait_ge(s_small, 48)
                c.link(dve.tensor_scalar(silu[:], silu[:], 1.0, None, ALU.add))
                c.link(dve.reciprocal(silu[:], silu[:]))
                dve.tensor_tensor(silu[:], silu[:], cond[:], ALU.mult).then_inc(s_silu, 1)
                for j in range(RING):
                    dve.sem_inc(s_free[j], 1)
                with dve.Fori(0, NCH // RING) as r:
                    for j in range(RING):
                        dve.wait_ge(s_mm, r * RING + (j + 1))
                        o = r * (RING * CH) + j * CH
                        dve.tensor_tensor(mod[:, bass.ds(o, CH)], acc[j][0:COND, :], mod[:, bass.ds(o, CH)],
                                          ALU.add).then_inc(s_free[j], 1)
                dve.wait_ge(s_sq, TILES)
                dve.tensor_scalar(g.rstd[:], ss[:], 1.0 / D, EPS, ALU.mult, ALU.add).then_inc(s_ms, 1)
                dve.wait_ge(s_rt, 1)
                c.link(dve.reciprocal(g.rstd[:], g.rstd[:]))
                dve.wait_ge(s_col, 1)
                for i in range(2):
                    c.link(dve.tensor_copy(g.shift[:, i], colT[:, 2 * i]))
                    c.link(dve.tensor_scalar(g.scale[:, i], colT[:, 2 * i + 1], 1.0, None, ALU.add))
                    c.link(dve.tensor_tensor(g.scale[:, i], g.scale[:, i],
                                             norms[:, i].unsqueeze(2).to_broadcast([P, KD, COND]), ALU.mult))
                n = 0
                for i in range(2):
                    for cnd in range(COND):
                        for half in range(2):
                            dve.wait_ge(s_row, n + 1)
                            dve.tensor_copy((g.gate1, g.gate2)[i][:, cnd, half * CH:(half + 1) * CH],
                                            rowB[n % 2][:]).then_inc(s_rowe, 1)
                            n += 1


def project_in(nc, g, io):
    with ExitStack() as ctx:
        def sb(name, shape, dt=F32):
            return ctx.enter_context(nc.sbuf_tensor(name, shape, dt))

        def sem(name):
            return ctx.enter_context(nc.semaphore(name))

        def psum(name):
            return ctx.enter_context(nc.psum_tensor(name, [P, 512], F32))

        xn = sb("in_xn", [P, D])
        hT = sb("in_hT", [P, KD, P])
        trig = sb("in_trig", [P, 2 * ADH])
        heads = sb("in_heads", [P, QKH * ADH + AKV * ADH + 4 * MH])
        sqh = sb("in_sqh", [P, QKH * ADH])
        turned = sb("in_turned", [P, QKH * ADH])
        rms = sb("in_rms", [P, QKH])
        g10 = sb("in_g10", [P, QKH * ADH])
        bg = sb("in_bg", [P, 4 * MH])
        kdup = sb("in_kdup", [P, AKV, 2, ADH])
        gates = sb("in_gates", [P, P])
        kv = sb("in_kv", [P, 2 * MW])
        q = sb("in_q", [P, MW])
        qkT = sb("in_qkT", [P, 2 * MW])
        aqT = sb("in_aqT", [P, 512])

        xTp = [psum("in_xT0"), psum("in_xT1")]
        zp = [psum(f"in_z{i}") for i in range(3)]
        aqTp = psum("in_aqTp")
        akTp = psum("in_akTp")

        s_small = sem("in_small_in")
        s_x = sem("in_x_in")
        s_xn = sem("in_xn_ready")
        s_trig = sem("in_trig_in")
        s_xT = sem("in_xT_done")
        s_hT0 = sem("in_hT_dve")
        s_hT1 = sem("in_hT_act")
        s_z = sem("in_z_done")
        s_zd = sem("in_z_out_dve")
        s_za = sem("in_z_out_act")
        s_mid = sem("in_dve_chain")
        s_rt_in = sem("in_meansq_done")
        s_rt = sem("in_sqrt_done")
        s_swap = sem("in_swap_done")
        s_normed = sem("in_normed")
        s_rope = sem("in_rope_done")
        s_att = sem("in_att_ready")
        s_qkT = sem("in_qkT_done")
        s_attT = sem("in_attT_done")
        s_attTd = sem("in_attT_out_dve")
        s_kv_out = sem("in_kv_stored")
        s_qkTe = sem("in_qkT_out")
        s_qkT_out = sem("in_qkT_stored")
        s_aqTe = sem("in_aqT_out")
        s_aqT_out = sem("in_aqT_stored")
        s_pad = sem("in_pads_zeroed")
        MID = 6

        with nc.Block() as block:
            @block.sync
            def _(sp):
                sp.dma_start(g10[:], io.head_norm).then_inc(s_small, 16)
                sp.dma_start(bg[:], io.b_gates).then_inc(s_small, 16)

                def load(t, first=False):
                    if not first:
                        sp.wait_ge(s_xT, t)
                    sp.dma_start(xn[:], io.x[t]).then_inc(s_x, 16)
                    if not first:
                        sp.wait_ge(s_rope, t)
                    sp.dma_start(trig[:], io.trig[t]).then_inc(s_trig, 16)

                load(0, True)
                with sp.Fori(1, TILES) as t:
                    load(t)

            @block.gpsimd
            def _(pool):
                pool.memset(gates[:], 0.0).then_inc(s_small, 1)

                def tile(t):
                    pool.wait_ge(s_x, t * 16 + 16)
                    pool.tensor_tensor(xn[:], xn[:], g.rstd[:, bass.ds(t, 1)].to_broadcast([P, D]),
                                       ALU.mult).then_inc(s_xn, 1)
                    pool.wait_ge(s_normed, t + 1)
                    pool.sem_inc(g.s_tick, 1)
                    src = heads[:, 0:QKH * ADH].rearrange("p (h s c) -> p h s c", s=2, c=ADH // 4)
                    dst = turned[:].rearrange("p (h s c) -> p h s c", s=2, c=ADH // 4)
                    pool.tensor_copy(dst[:, :, 0, :], src[:, :, 1, :])
                    pool.tensor_copy(dst[:, :, 1, :], src[:, :, 0, :]).then_inc(s_swap, 1)

                tile(0)
                with pool.Fori(1, TILES) as t:
                    tile(t)

            @block.tensor
            def _(pe):
                pe.wait_ge(g.s_w_in, 16 * KD)

                def tile(t, first=False):
                    pe.wait_ge(s_xn, t + 1)
                    if not first:
                        pe.wait_ge(s_qkTe, t * 2)
                    for k in range(KD):
                        mm = pe.transpose(xTp[k // 4][:, (k % 4) * P:(k % 4 + 1) * P], xn[:, k * P:(k + 1) * P], g.ident[:])
                    mm.then_inc(s_xT, 1)
                    pe.wait_ge(s_hT0, t + 1)
                    pe.wait_ge(s_hT1, t + 1)
                    for b, (c0, n) in enumerate(((C_A, 512), (C_R, REST), (C_Q, 512), (C_K, 512), (C_V, 512), (C_O, 512))):
                        if b >= 3 or not first:
                            if b < 2:
                                pe.wait_ge(s_za, t * 4 - 2 + b)
                            elif b == 2:
                                pe.wait_ge(s_za, t * 4)
                            elif b < 5:
                                pe.wait_ge(s_zd, t * 2 + (b - 2))
                            else:
                                pe.wait_ge(s_za, t * 4 + 1)
                        for k in range(KD):
                            mm = pe.matmul(zp[b % 3][:, 0:n], hT[:, k, :], g.w_in[:, k, c0:c0 + n],
                                           start=(k == 0), stop=(k == KD - 1))
                        mm.then_inc(s_z, 1)
                    for i in range(2):
                        pe.wait_ge(s_za, t * 4 + (i + 1))
                        for h in range(MH):
                            src = q[:, h * P:(h + 1) * P] if i == 0 else kv[:, h * P:(h + 1) * P]
                            mm = pe.transpose(xTp[i][:, h * P:(h + 1) * P], src, g.ident[:])
                        mm.then_inc(s_qkT, 1)
                    pe.wait_ge(s_att, t + 1)
                    if not first:
                        pe.wait_ge(s_aqTe, t)
                        pe.wait_ge(s_attTd, t)
                    for h in range(AH // 2):
                        pe.transpose(aqTp[:, h * P:(h + 1) * P], heads[:, h * P:(h + 1) * P], g.ident[:])
                    for h in range(AKV):
                        pe.transpose(akTp[:, h * P:(h + 1) * P], kdup[:, h].rearrange("p a d -> p (a d)"), g.ident[:])
                    pe.transpose(akTp[:, 2 * P:3 * P], gates[:], g.ident[:]).then_inc(s_attT, 1)

                tile(0, True)
                with pe.Fori(1, TILES) as t:
                    tile(t)

            @block.scalar
            def _(act):
                def tile(t, cnd, first=False):
                    act.wait_ge(s_xT, t + 1)
                    if not first:
                        act.wait_ge(s_z, t * 6)
                    for k in range(4, KD):
                        last = act.activation(hT[:, k, :], xTp[1][:, (k - 4) * P:(k - 3) * P], ACT.Identity,
                                              bias=g.shift[:, 0, k, cnd:cnd + 1], scale=g.scale[:, 0, k, cnd:cnd + 1])
                    last.then_inc(s_hT1, 1)
                    act.wait_ge(s_rt_in, t + 1)
                    act.activation(rms[:], rms[:], ACT.Sqrt).then_inc(s_rt, 1)
                    act.wait_ge(s_z, t * 6 + 3)
                    if not first:
                        act.wait_ge(s_qkT, t * 2)
                        act.wait_ge(s_kv_out, t * 16)
                    act.activation(q[:], zp[2][:], ACT.Copy, scale=float(P) ** -0.5).then_inc(s_za, 1)
                    act.wait_ge(s_z, t * 6 + 4)
                    act.activation(kv[:, 0:MW], zp[0][:], ACT.Copy).then_inc(s_za, 1)
                    act.wait_ge(s_z, t * 6 + 5)
                    act.activation(kv[:, MW:2 * MW], zp[1][:], ACT.Copy).then_inc(s_za, 1)
                    act.wait_ge(s_z, t * 6 + 6)
                    act.activation(g.mo[:, t, :], zp[2][:], ACT.Copy).then_inc(s_za, 1)
                    act.wait_ge(s_za, t * 4 + 3)
                    act.dma_start(g.kv_dram[t], kv[:]).then_inc(s_kv_out, 16)
                    if not first:
                        act.wait_ge(s_qkT_out, t * 16)
                        act.wait_ge(s_aqT_out, t * 16)
                    for i in range(2):
                        act.wait_ge(s_qkT, t * 2 + (i + 1))
                        act.activation(qkT[:, i * MW:(i + 1) * MW], xTp[i][:], ACT.Copy).then_inc(s_qkTe, 1)
                    act.wait_ge(s_qkTe, t * 2 + 2)
                    act.dma_start(g.qkT_dram[t], qkT[:]).then_inc(s_qkT_out, 16)
                    act.wait_ge(s_attT, t + 1)
                    act.activation(aqT[:], aqTp[:], ACT.Copy).then_inc(s_aqTe, 1)
                    act.wait_ge(s_aqTe, t + 1)
                    act.dma_start(g.aqT_dram[t], aqT[:]).then_inc(s_aqT_out, 16)

                tile(0, 0, True)
                with act.Fori(1, TILES) as t:
                    tile(t, 1)
                act.wait_ge(s_kv_out, 16 * TILES)
                act.wait_ge(s_qkT_out, 16 * TILES)
                act.wait_ge(s_aqT_out, 16 * TILES)

            @block.vector
            def _(dve):
                dve.wait_ge(s_small, 33)
                dve.memset(g.akT[:], 0.0).then_inc(s_pad, 1)
                dve.memset(g.av[:], 0.0).then_inc(s_pad, 1)
                dve.wait_ge(s_pad, 2)

                def tile(t, cnd, first=False):
                    c = Count(dve, s_mid, MID, t)
                    dve.wait_ge(s_xT, t + 1)
                    if not first:
                        dve.wait_ge(s_z, t * 6)
                    for k in range(4):
                        last = dve.tensor_scalar(hT[:, k, :], xTp[0][:, k * P:(k + 1) * P], g.scale[:, 0, k, cnd:cnd + 1],
                                                 g.shift[:, 0, k, cnd:cnd + 1], ALU.mult, ALU.add)
                    last.then_inc(s_hT0, 1)
                    NQ = AH * ADH
                    NK = QKH * ADH
                    dve.wait_ge(s_z, t * 6 + 1)
                    if not first:
                        dve.wait_ge(s_attT, t)
                    dve.tensor_copy(heads[:, 0:NQ], zp[0][:]).then_inc(s_zd, 1)
                    dve.wait_ge(s_z, t * 6 + 2)
                    dve.tensor_copy(heads[:, NQ:NQ + REST], zp[1][:, 0:REST]).then_inc(s_zd, 1)
                    dve.wait_ge(s_zd, t * 2 + 2)
                    c.link(dve.tensor_tensor(sqh[:], heads[:, 0:NK], heads[:, 0:NK], ALU.mult))
                    hv = heads[:, 0:NK].rearrange("p (h d) -> p h d", d=ADH)
                    c.link(dve.tensor_reduce(rms[:], sqh[:].rearrange("p (h d) -> p h d", d=ADH), AX.X, ALU.add))
                    dve.tensor_scalar(rms[:], rms[:], 1.0 / ADH, EPS, ALU.mult, ALU.add).then_inc(s_rt_in, 1)
                    dve.wait_ge(s_rt, t + 1)
                    c.link(dve.reciprocal(rms[:], rms[:]))
                    c.link(dve.tensor_tensor(hv, hv, rms[:].unsqueeze(2).to_broadcast([P, QKH, ADH]), ALU.mult))
                    dve.tensor_tensor(heads[:, 0:NK], heads[:, 0:NK], g10[:], ALU.mult).then_inc(s_normed, 1)
                    dve.wait_ge(s_normed, t + 1)
                    if first:
                        dve.tensor_copy(g.new_kv[:], heads[:, NQ:NQ + 2 * AKV * ADH]).then_inc(g.s_new_kv, 1)
                        dve.wait_ge(g.s_new_kv, 1)
                    dve.wait_ge(s_swap, t + 1)
                    dve.wait_ge(s_trig, t * 16 + 16)
                    cos = trig[:, 0:ADH].unsqueeze(1).to_broadcast([P, QKH, ADH])
                    sin = trig[:, ADH:2 * ADH].unsqueeze(1).to_broadcast([P, QKH, ADH])
                    tv = turned[:].rearrange("p (h d) -> p h d", d=ADH)
                    c.link(dve.tensor_tensor(hv, hv, cos, ALU.mult))
                    c.link(dve.tensor_tensor(tv, tv, sin, ALU.mult))
                    last = dve.tensor_tensor(heads[:, 0:NK], heads[:, 0:NK], turned[:], ALU.add)
                    last.then_inc(s_rope, 1)
                    dve.wait_ge(s_rope, t + 1)
                    for a in range(2):
                        dve.tensor_copy(kdup[:, :, a, :], heads[:, NQ:NK].rearrange("p (g d) -> p g d", d=ADH))
                    dve.tensor_copy(g.av[:, t + 1, :], heads[:, NK:NK + AKV * ADH])
                    gv = gates[:].rearrange("p (a r) -> p a r", a=4)[:, :, 0:MH]
                    dve.tensor_tensor(gv, heads[:, NK + AKV * ADH:].rearrange("p (a r) -> p a r", a=4),
                                      bg[:].rearrange("p (a r) -> p a r", a=4), ALU.add).then_inc(s_att, 1)
                    dve.wait_ge(s_attT, t + 1)
                    dve.tensor_copy(g.akT[:, :, bass.ds(t * P + P, P)], akTp[:, 0:2 * P].rearrange("p (g n) -> p g n", g=2))
                    for i in range(4):
                        last = dve.tensor_copy(g.grow[i][:, bass.ds(t * P, P)], akTp[32 * i:32 * i + MH, 2 * P:3 * P])
                    last.then_inc(s_attTd, 1)

                tile(0, 0, True)
                with dve.Fori(1, TILES) as t:
                    tile(t, 1)


def mlstm(nc, g, io):
    ROW = TILES * P
    with ExitStack() as ctx:
        def sb(name, shape, dt=F32):
            return ctx.enter_context(nc.sbuf_tensor(name, shape, dt))

        def sem(name):
            return ctx.enter_context(nc.semaphore(name))

        def psum(name, shape):
            return ctx.enter_context(nc.psum_tensor(name, shape, F32))

        keep = sb("ml_keep", [MH, ROW])
        cum = [sb(f"ml_cum{d}", [MH, ROW]) for d in range(2)]
        mx = [sb(f"ml_max{d}", [MH, ROW]) for d in range(2)]
        negM = cum
        inter = [sb(f"ml_inter{d}", [MH, ROW]) for d in range(2)]
        mprev = [sb(f"ml_mprev{d}", [MH, TILES]) for d in range(2)]
        m0 = sb("ml_m0", [MH, 2])
        rows = [sb(f"ml_rows{d}", [P, ROW]) for d in range(2)]
        rfix = [sb(f"ml_rfix{d}", [P, P]) for d in range(2)]
        qkT = [sb(f"ml_qkT{d}", [P, 2 * MH, P]) for d in range(2)]
        kk = [sb(f"ml_k{d}", [P, MH, P]) for d in range(2)]
        v1 = [sb(f"ml_v{d}", [P, MH, C1]) for d in range(2)]
        gk = [sb(f"ml_gk{d}", [P, MH, P]) for d in range(2)]
        cols = [sb(f"ml_cols{d}", [P, 5, MH]) for d in range(2)]
        ew = [sb(f"ml_e{d}", [P, MH, P]) for d in range(2)]
        sT = [sb(f"ml_s{d}", [P, MH, P]) for d in range(2)]
        num = [sb(f"ml_num{d}", [P, MH, C1]) for d in range(2)]
        den = [sb(f"ml_den{d}", [P, MH]) for d in range(2)]
        c_new = [sb(f"ml_cnew{d}", [P, MH, C1]) for d in range(2)]
        c_run = [sb(f"ml_crun{d}", [P, MH, C1]) for d in range(2)]

        misc = psum("ml_misc", [P, 512])
        eP = psum("ml_eP", [P, MH, P])
        qkP = psum("ml_qkP", [P, MH, P])
        iP = [psum(f"ml_iP{i}", [P, 2, 256]) for i in range(2)]
        oP = [psum(f"ml_oP{i}", [P, 2, 256]) for i in range(2)]
        cP = psum("ml_cP", [P, 2, 256])

        s_in = sem("ml_small_in")
        s_ld = [sem(f"ml_load{d}") for d in range(2)]
        s_abs = sem("ml_abs")
        s_exp = sem("ml_exp")
        s_ln = sem("ml_ln")
        s_dve = sem("ml_dve_rows")
        s_rows = sem("ml_rows_ready")
        s_ones = sem("ml_ones_ready")
        s_r = sem("ml_rfix_ready")
        s_col = sem("ml_colT_done")
        s_cols = sem("ml_cols_ready")
        s_gk = sem("ml_gk_ready")
        s_eP = sem("ml_eP_done")
        s_e = sem("ml_e_ready")
        s_qk = sem("ml_qk_done")
        s_s = sem("ml_s_ready")
        s_i = sem("ml_inter_done")
        s_t = sem("ml_inter_scaled")
        s_o = sem("ml_intra_done")
        s_n = sem("ml_num_ready")
        s_c = sem("ml_c_done")
        s_cn = sem("ml_c_updated")
        s_mid = sem("ml_dve_chain")
        s_h = sem("ml_h_ready")
        s_out = sem("ml_state_stored")
        MID = 3

        with nc.Block() as block:
            def tiles(t):
                return (t, 0 if isinstance(t, int) else TILES - t)

            @block.sync
            def _(sp):
                sp.dma_start(m0[:], io.m0).then_inc(s_in, 16)
                for d in range(2):
                    sp.dma_start(c_run[d][:], io.c0[d]).then_inc(s_in, 16)

                def load(t, first=False):
                    for d in range(2):
                        ti = tiles(t)[d]
                        if not first:
                            sp.wait_ge(s_o, t * 4 - 2 + 2 * d)
                            sp.wait_ge(s_gk, t * 2 - 1 + d)
                            sp.sem_inc(g.s_tick, 1)
                        sp.dma_start(qkT[d][:].rearrange("p h n -> p (h n)"), g.qkT_dram[ti]).then_inc(s_ld[d], 16)
                        sp.dma_start(kk[d][:].rearrange("p h n -> p (h n)"), g.kv_dram[ti, :, 0:MW]).then_inc(s_ld[d], 16)
                        sp.dma_start(v1[d][:, :, 0:P], g.kv_dram[ti, :, MW:2 * MW].rearrange("p (h n) -> p h n", h=MH)
                                     ).then_inc(s_ld[d], 16)

                load(0, True)
                sp.wait_ge(s_cn, 8)
                for d in range(2):
                    sp.dma_start(io.new_c[d], c_new[d][:]).then_inc(s_out, 16)
                    end = P - 1 if d == 0 else 0
                    sp.dma_start(io.new_m[d], mx[d][:, end:end + 1]).then_inc(s_out, 16)
                sp.dma_start(io.new_kv, g.new_kv[:]).then_inc(s_out, 16)
                with sp.Fori(1, TILES) as t:
                    load(t)
                sp.wait_ge(s_out, 80)

            @block.scalar
            def _(act):
                for d in range(2):
                    act.wait_ge(s_dve, 2 + d)
                    act.activation(cum[d][:], cum[d][:], ACT.Exp, scale=-1.0).then_inc(s_exp, 1)
                    act.wait_ge(s_exp, d + 1)
                    act.activation(cum[d][:], cum[d][:], ACT.Ln, bias=1.0).then_inc(s_ln, 1)

                def step(t, first=False):
                    for d in range(2):
                        u = t * 2 + d
                        act.wait_ge(s_col, u + 1)
                        if not first:
                            act.wait_ge(s_h, u - 1)
                            act.wait_ge(s_gk, u - 1)
                        act.activation(cols[d][:, 0, :], misc[:, 0:MH], ACT.Copy)
                        act.activation(cols[d][:, 1:4, :], misc[:, 32:P].rearrange("p (a r) -> p a r", a=3)[:, :, 0:MH], ACT.Exp)
                        act.activation(cols[d][:, 4, :], misc[:, P:P + MH], ACT.Exp).then_inc(s_cols, 1)
                        act.wait_ge(s_cols, u + 1)
                        act.wait_ge(s_eP, u + 1)
                        for h in range(MH):
                            last = act.activation(ew[d][:, h, :], eP[:, h, :], ACT.Exp, bias=cols[d][:, 0, h:h + 1])
                        last.then_inc(s_e, 1)
                        for p in range(2):
                            act.wait_ge(s_i, u * 2 + (p + 1))
                            for j in range(2):
                                h = 2 * p + j
                                last = act.activation(num[d][:, h, :], iP[p][:, j, 0:C1], ACT.Copy,
                                                      scale=cols[d][:, 1, h:h + 1])
                            last.then_inc(s_t, 1)

                step(0, True)
                with act.Fori(1, TILES) as t:
                    step(t)

            @block.gpsimd
            def _(pool):
                for d in range(2):
                    pool.memset(v1[d][:, :, P:C1], 1.0)
                pool.memset(c_new[0][:], 0.0)
                pool.memset(c_new[1][:], 0.0).then_inc(s_ones, 1)
                pool.wait_ge(s_rows, 2)

                def step(t, first=False):
                    for d in range(2):
                        u = t * 2 + d
                        if not first:
                            pool.wait_ge(s_col, u - 1)
                            pool.sem_inc(g.s_tick, 1)
                        pool.tensor_copy(rfix[d][:], rows[d][:, bass.ds(tiles(t)[d] * P, P)]).then_inc(s_r, 1)
                    for d in range(2):
                        u = t * 2 + d
                        pool.wait_ge(s_cols, u + 1)
                        pool.wait_ge(s_ld[d], t * 48 + 48)
                        if not first:
                            pool.wait_ge(s_c, u * 2 - 2)
                        pool.tensor_tensor(gk[d][:], kk[d][:], cols[d][:, 3, :].unsqueeze(2).to_broadcast([P, MH, P]),
                                           ALU.mult).then_inc(s_gk, 1)

                step(0, True)
                with pool.Fori(1, TILES) as t:
                    step(t)

            @block.tensor
            def _(pe):
                pe.wait_ge(s_ones, 1)
                pe.wait_ge(s_rows, 2)
                pe.wait_ge(s_in, 48)

                def step(t, state, first=False):
                    for d in range(2):
                        u = t * 2 + d
                        new = first and d == 0
                        ti = tiles(t)[d]
                        end = P - 1 if d == 0 else 0
                        pe.wait_ge(s_r, u + 1)
                        if not new:
                            pe.wait_ge(s_cols, u)
                        pe.transpose(misc[:, 0:P], rfix[d][:], g.ident[:])
                        for h in range(MH):
                            mm = pe.matmul(misc[:, P + h:P + h + 1], g.sel[:, h, :], inter[d][:, bass.ds(ti * P + end, 1)],
                                           start=True, stop=True)
                        mm.then_inc(s_col, 1)
                        if not new:
                            pe.wait_ge(s_e, u)
                        for h in range(MH):
                            pe.matmul(eP[:, h, :], g.sel[:, h, :], negM[d][:, bass.ds(ti * P, P)], start=(h == 0), stop=False)
                        mask = g.neg_after if d == 0 else g.neg_before
                        pe.matmul(eP[:].rearrange("p h n -> p (h n)"), g.ident[:], mask[:].rearrange("p h n -> p (h n)"),
                                  start=False, stop=True).then_inc(s_eP, 1)
                        pe.wait_ge(s_ld[d], t * 48 + 48)
                        if not new:
                            pe.wait_ge(s_s, u)
                        for h in range(MH):
                            mm = pe.matmul(qkP[:, h, :], qkT[d][:, MH + h, :], qkT[d][:, h, :], start=True, stop=True)
                        mm.then_inc(s_qk, 1)
                        if not first:
                            pe.wait_ge(s_cn, u * 4 - 4)
                        for p in range(2):
                            if not new:
                                pe.wait_ge(s_t, u * 2 - 1 + p)
                            for j in range(2):
                                h = 2 * p + j
                                mm = pe.matmul(iP[p][:, j, 0:C1], qkT[d][:, h, :], state[d][:, h, :], start=True, stop=True)
                            mm.then_inc(s_i, 1)
                        for p in range(2):
                            pe.wait_ge(s_gk, u + 1)
                            if not (new and p == 0):
                                pe.wait_ge(s_cn, u * 4 + 2 * p)
                            for j in range(2):
                                h = 2 * p + j
                                mm = pe.matmul(cP[:, j, 0:C1], gk[d][:, h, :], v1[d][:, h, :], start=True, stop=True)
                            mm.then_inc(s_c, 1)
                            pe.wait_ge(s_s, u + 1)
                            if not new:
                                pe.wait_ge(s_n, u * 2 - 1 + p)
                            for j in range(2):
                                h = 2 * p + j
                                mm = pe.matmul(oP[p][:, j, 0:C1], sT[d][:, h, :], v1[d][:, h, :], start=True, stop=True)
                            mm.then_inc(s_o, 1)

                step(0, c_new, True)
                with pe.Fori(1, TILES) as t:
                    step(t, c_run)

            @block.vector
            def _(dve):
                c = Count(dve, s_dve)
                c.link(dve.memset(mprev[0][:], NEG))
                for d in range(2):
                    lf = g.grow[2 * d + 1]
                    c.link(dve.scalar_tensor_tensor(cum[d][:], lf[:], -1.0, lf[:], ALU.mult, ALU.max))
                c.link(dve.memset(mprev[1][:], NEG))
                for d in range(2):
                    c.link(dve.memset(rows[d][:], 0.0))
                c.link(dve.memset(keep[:], 1.0))
                c.link(dve.memset(keep[:].rearrange("h (c n) -> h c n", n=P)[:, :, 0:1], 0.0))
                dve.wait_ge(s_in, 48)
                for d in range(2):
                    li, lf = g.grow[2 * d], g.grow[2 * d + 1]
                    end = P - 1 if d == 0 else 0

                    def run(a, lo, hi):
                        return a[:, lo:hi] if d == 0 else a[:, lo:hi][:, ::-1]

                    def chunks(a):
                        return a.rearrange("h (c n) -> h c n", n=P)

                    dve.wait_ge(s_ln, d + 1)
                    c.link(dve.scalar_tensor_tensor(lf[:], lf[:], 0.0, cum[d][:], ALU.min, ALU.subtract))
                    c.link(dve.tensor_tensor_scan(run(cum[d], 0, ROW), keep[:], run(lf, 0, ROW), 0.0,
                                                  ALU.mult, ALU.add))
                    c.link(dve.tensor_tensor_scan(run(mx[d], 0, P), run(lf, 0, P), run(li, 0, P), NEG, ALU.add, ALU.max))
                    c.link(dve.tensor_tensor_scan(run(mx[d], P, ROW), run(lf, P, ROW), run(li, P, ROW), m0[:, d:d + 1],
                                                  ALU.add, ALU.max))
                    seed = 1 if d == 0 else TILES - 1
                    c.link(dve.tensor_copy(mprev[d][:, seed:seed + 1], m0[:, d:d + 1]))
                    ends = chunks(mx[d][:])[:, :, end]
                    if d == 0:
                        c.link(dve.tensor_copy(mprev[d][:, 2:TILES], ends[:, 1:TILES - 1]))
                    else:
                        c.link(dve.tensor_copy(mprev[d][:, 1:TILES - 1], ends[:, 2:TILES]))
                    c.link(dve.tensor_tensor(rows[d][0:MH, :], li[:], cum[d][:], ALU.subtract))
                    c.link(dve.tensor_tensor(negM[d][:], cum[d][:], mx[d][:], ALU.subtract))
                    c.link(dve.tensor_tensor(chunks(inter[d][:]), chunks(negM[d][:]),
                                             mprev[d][:].unsqueeze(2).to_broadcast([MH, TILES, P]), ALU.add))
                    dve.tensor_copy(rows[d][32:32 + MH, :], inter[d][:])
                    dve.tensor_scalar(rows[d][64:64 + MH, :], mx[d][:], -1.0, None, ALU.mult)
                    last_negM = chunks(negM[d][:])[:, :, end:end + 1].to_broadcast([MH, TILES, P])
                    dve.tensor_tensor(chunks(rows[d][96:96 + MH, :]), chunks(rows[d][0:MH, :]), last_negM,
                                      ALU.add).then_inc(s_rows, 1)

                def step(t, state, first=False):
                    for d in range(2):
                        u = t * 2 + d
                        cc = Count(dve, s_mid, MID, u, g.s_tick)
                        ti = tiles(t)[d]
                        dve.wait_ge(s_qk, u + 1)
                        dve.wait_ge(s_e, u + 1)
                        if not first:
                            dve.wait_ge(s_o, u * 2 - 2)
                        dve.tensor_tensor(sT[d][:], qkP[:], ew[d][:], ALU.mult).then_inc(s_s, 1)
                        for p in range(2):
                            dve.wait_ge(s_c, u * 2 + (p + 1))
                            dve.wait_ge(s_cols, u + 1)
                            for j in range(2):
                                h = 2 * p + j
                                dve.scalar_tensor_tensor(state[d][:, h, :], state[d][:, h, :], cols[d][:, 4, h:h + 1],
                                                         cP[:, j, 0:C1], ALU.mult, ALU.add).then_inc(s_cn, 1)
                            dve.wait_ge(s_t, u * 2 + (p + 1))
                            dve.wait_ge(s_o, u * 2 + (p + 1))
                            nv = num[d][:, 2 * p:2 * p + 2, :]
                            dve.tensor_tensor(nv, nv, oP[p][:, :, 0:C1], ALU.add).then_inc(s_n, 1)
                        dve.wait_ge(s_n, u * 2 + 2)
                        cc.link(dve.scalar_tensor_tensor(den[d][:], num[d][:, :, P], -1.0, num[d][:, :, P], ALU.mult, ALU.max))
                        cc.link(dve.tensor_tensor(den[d][:], den[d][:], cols[d][:, 2, :], ALU.max))
                        cc.link(dve.reciprocal(den[d][:], den[d][:]))
                        dve.tensor_tensor(g.h_dir[d][:, ti, :].rearrange("p (h n) -> p h n", h=MH), num[d][:, :, 0:P],
                                          den[d][:].unsqueeze(2).to_broadcast([P, MH, P]), ALU.mult).then_inc(s_h, 1)

                step(0, c_new, True)
                with dve.Fori(1, TILES) as t:
                    step(t, c_run)


def attend(nc, g, io):
    with ExitStack() as ctx:
        def sb(name, shape, dt=F32):
            return ctx.enter_context(nc.sbuf_tensor(name, shape, dt))

        def sem(name):
            return ctx.enter_context(nc.semaphore(name))

        def psum(name):
            return ctx.enter_context(nc.psum_tensor(name, [P, 512], F32))

        w_out = sb("at_w_out", [P, KD, D])
        qT = sb("at_qT", [P, AH // 2, P])
        mask = sb("at_mask", [P, 4 * P])
        x = sb("at_x", [P, D])
        kw = sb("at_window_kT", [P, AKV, 3 * P])
        ckT = sb("at_cache_kT", [P, AKV, P])
        cv = sb("at_cache_v", [P, AKV * ADH])
        sink = sb("at_sink", [P, AH])
        mhg = sb("at_mh_g", [P, MW])
        s = [sb(f"at_s{i}", [P, 4 * P]) for i in range(2)]
        p = [sb(f"at_p{i}", [P, 4 * P]) for i in range(2)]
        pT = [sb(f"at_pT{i}", [P, 4 * P]) for i in range(2)]
        mxs = sb("at_max", [P, AH])
        nmx = sb("at_negmax", [P, AH])
        rs = sb("at_sum", [P, AH])
        es = sb("at_sink_exp", [P, AH])
        hs = sb("at_h", [P, MW])
        hq = sb("at_hsq", [P, MW])
        sg = sb("at_sigmoid", [P, MW])
        hr = sb("at_hrms", [P, MH])
        mix = sb("at_mix", [P, D])
        mixT = sb("at_mixT", [P, KD, P])
        x1 = sb("at_x1", [P, D])
        xn = sb("at_xn", [P, D])
        ss = sb("at_ss", [P, 1])
        h2T = sb("at_h2T", [P, KD, P])
        h2 = xn

        sP = [psum(f"at_sP{i}") for i in range(2)]
        tP = [psum(f"at_tP{i}") for i in range(2)]
        aP = psum("at_aP")
        uP = [psum(f"at_uP{i}") for i in range(3)]

        s_small = sem("at_small_in")
        s_wo = sem("at_w_out_in")
        s_q = sem("at_q_in")
        s_kw = sem("at_window_keys_ready")
        s_x = sem("at_x_in")
        s_sc = sem("at_scores_done")
        s_s = sem("at_s_ready")
        s_nm = sem("at_negmax_ready")
        s_p = sem("at_p_ready")
        s_pTp = sem("at_p_turned")
        s_pT = sem("at_pT_ready")
        s_pv = sem("at_pv_done")
        s_pool = sem("at_pool_chain")
        s_hs = sem("at_h_squared")
        s_hm = sem("at_h_meansq")
        s_hrt = sem("at_h_sqrt")
        s_sge = sem("at_gate_exp")
        s_hr = sem("at_h_rms_ready")
        s_mixm = sem("at_mix_mlstm")
        s_dif = sem("at_sink_diff")
        s_es = sem("at_sink_exp_done")
        s_mixa = sem("at_mix_attn")
        s_mT = sem("at_mix_turned")
        s_mTa = sem("at_mixT_act")
        s_mTd = sem("at_mixT_dve")
        s_wo_mm = sem("at_w_out_done")
        s_x1 = sem("at_x1_ready")
        s_sq = sem("at_x1_squared")
        s_ms = sem("at_x1_meansq")
        s_rt = sem("at_x1_sqrt")
        s_xn = sem("at_xn_ready")
        s_xT = sem("at_xn_turned")
        s_hTa = sem("at_h2T_act")
        s_hTd = sem("at_h2T_dve")
        s_h2p = sem("at_h2_turned")
        s_h2a = sem("at_h2_act")
        s_h2d = sem("at_h2_dve")
        s_x1o = sem("at_x1_stored")
        s_h2o = sem("at_h2_stored")
        s_front = sem("at_dve_front_chain")
        s_tail = sem("at_dve_tail_chain")
        FRONT, TAIL = 5, 3
        POOLS = 3

        def interleave(t, front, tail):
            work = iter(()) if isinstance(t, int) and t == 0 else tail
            if not (isinstance(t, int) and t == TILES):
                front(t, work)
            for _ in work:
                pass

        def run(eng, front, tail):
            interleave(0, front, None)
            interleave(1, front, tail(0, 0))
            with eng.Fori(2, TILES) as t:
                interleave(t, front, tail(t - 1, 1))
            interleave(TILES, front, tail(TILES - 1, 1))

        with nc.Block() as block:
            @block.sync
            def _(sp):
                for dst, src in ((ckT, io.cache_kT), (cv, io.cache_v), (sink, io.sink), (mhg, io.mh_g)):
                    sp.dma_start(dst[:], src).then_inc(s_small, 16)

                def load(t, first=False):
                    if not first:
                        sp.wait_ge(s_sc, t * AH)
                        sp.wait_ge(s_s, t * AH)
                    sp.dma_start(qT[:].rearrange("p h n -> p (h n)"), g.aqT_dram[t]).then_inc(s_q, 16)
                    sp.dma_start(mask[:], io.att_mask[t]).then_inc(s_q, 16)

                load(0, True)
                sp.dma_start(x[:], io.x[0]).then_inc(s_x, 16)
                for k in range(KD):
                    sp.dma_start(w_out[:, k, :], io.w_out[k * P:(k + 1) * P, :]).then_inc(s_wo, 16)
                with sp.Fori(1, TILES) as t:
                    load(t)
                    sp.wait_ge(s_x1, t * 2)
                    sp.dma_start(g.x1_dram[t - 1], x1[:]).then_inc(s_x1o, 16)
                    sp.dma_start(x[:], io.x[t]).then_inc(s_x, 16)
                sp.wait_ge(s_x1, TILES * 2)
                sp.dma_start(g.x1_dram[TILES - 1], x1[:]).then_inc(s_x1o, 16)
                sp.wait_ge(s_x1o, TILES * 16)

            @block.gpsimd
            def _(pool):
                pool.wait_ge(s_small, 64)

                def tile(t, first=False):
                    c = Count(pool, s_pool, POOLS, t)
                    if not first:
                        pool.wait_ge(s_mixm, t)
                        pool.wait_ge(s_sc, t * AH)
                    pool.tensor_copy(kw[:], g.akT[:, :, bass.ds(t * P, 3 * P)]).then_inc(s_kw, 1)
                    c.link(pool.tensor_tensor(hs[:], g.h_dir[0][:, t, :], g.h_dir[1][:, t, :], ALU.add))
                    pool.tensor_tensor(hq[:], hs[:], hs[:], ALU.mult).then_inc(s_hs, 1)
                    pool.wait_ge(s_hr, t + 1)
                    hv = hs[:].rearrange("p (h n) -> p h n", h=MH)
                    c.link(pool.tensor_tensor(hv, hv, hr[:].unsqueeze(2).to_broadcast([P, MH, P]), ALU.mult))
                    c.link(pool.tensor_tensor(hs[:], hs[:], mhg[:], ALU.mult))
                    if not first:
                        pool.wait_ge(s_mT, t)
                    pool.tensor_tensor(mix[:, 0:MW], hs[:], sg[:], ALU.mult).then_inc(s_mixm, 1)

                tile(0, True)
                with pool.Fori(1, TILES) as t:
                    tile(t)

            @block.tensor
            def _(pe):
                def front(t, work):
                    first = isinstance(t, int) and t == 0

                    def score(h):
                        if not (first and h < 2):
                            pe.wait_ge(s_s, t * AH + (h - 1))
                        lo = (h % 2) * ADH
                        grp = h // (AH // AKV)
                        lhs = qT[lo:lo + ADH, h // 2, :]
                        pe.matmul(sP[h % 2][:, 0:P], lhs, ckT[lo:lo + ADH, grp, :], start=True, stop=True)
                        pe.matmul(sP[h % 2][:, P:4 * P], lhs, kw[lo:lo + ADH, grp, :],
                                  start=True, stop=True).then_inc(s_sc, 1)

                    def values(h):
                        pe.wait_ge(s_p, t * AH + (h + 1))
                        if not (first and h < 2):
                            pe.wait_ge(s_pT, t * AH + (h - 1))
                        for j in range(4):
                            mm = pe.transpose(tP[h % 2][:, j * P:(j + 1) * P], p[h % 2][:, j * P:(j + 1) * P], g.ident[:])
                        mm.then_inc(s_pTp, 1)
                        pe.wait_ge(s_pT, t * AH + (h + 1))
                        if not first and h == 0:
                            pe.wait_ge(s_mixa, t)
                        c0 = (h // (AH // AKV)) * ADH
                        for j in range(4):
                            rhs = cv[:, c0:c0 + ADH] if j == 0 else g.av[:, t + (j - 1), c0:c0 + ADH]
                            mm = pe.matmul(aP[:, h * ADH:(h + 1) * ADH], pT[h % 2][:, j * P:(j + 1) * P], rhs,
                                           start=(j == 0), stop=(j == 3))
                        mm.then_inc(s_pv, 1)

                    pe.wait_ge(s_q, t * 32 + 32)
                    pe.wait_ge(s_kw, t + 1)
                    score(0)
                    for h in range(AH):
                        if h + 1 < AH:
                            score(h + 1)
                        values(h)
                        if h in (0, 1, 2, 6):
                            next(work, None)

                def tail(t, cnd):
                    first = isinstance(t, int) and t == 0
                    pe.wait_ge(s_mixm, t + 1)
                    pe.wait_ge(s_mixa, t + 1)
                    if not first:
                        pe.wait_ge(s_h2a, t)
                        pe.wait_ge(s_h2d, t)
                    for k in range(KD):
                        mm = pe.transpose(uP[k // 4][:, (k % 4) * P:(k % 4 + 1) * P], mix[:, k * P:(k + 1) * P], g.ident[:])
                    mm.then_inc(s_mT, 1)
                    yield
                    if first:
                        pe.wait_ge(s_wo, 16 * KD)
                    pe.wait_ge(s_mTa, t + 1)
                    pe.wait_ge(s_mTd, t + 1)
                    for half in range(2):
                        for k in range(KD):
                            mm = pe.matmul(uP[2 - 2 * half][:], mixT[:, k, :], w_out[:, k, half * 512:(half + 1) * 512],
                                           start=(k == 0), stop=(k == KD - 1))
                        mm.then_inc(s_wo_mm, 1)
                        yield
                    pe.wait_ge(s_xn, t + 1)
                    for k in range(KD):
                        mm = pe.transpose(uP[1 + k // 4][:, (k % 4) * P:(k % 4 + 1) * P], xn[:, k * P:(k + 1) * P], g.ident[:])
                    mm.then_inc(s_xT, 1)
                    yield
                    pe.wait_ge(s_hTa, t + 1)
                    pe.wait_ge(s_hTd, t + 1)
                    for k in range(KD):
                        mm = pe.transpose(uP[k // 4][:, (k % 4) * P:(k % 4 + 1) * P], h2T[:, k, :], g.ident[:])
                    mm.then_inc(s_h2p, 1)

                pe.wait_ge(s_small, 64)
                run(pe, front, tail)

            @block.scalar
            def _(act):
                def front(t, work):
                    first = isinstance(t, int) and t == 0
                    if not first:
                        act.wait_ge(s_mixm, t)
                    act.activation(sg[:], g.mo[:, t, :], ACT.Exp, scale=-1.0).then_inc(s_sge, 1)
                    for h in range(AH):
                        act.wait_ge(s_nm, t * AH + (h + 1))
                        if not (first and h < 2):
                            act.wait_ge(s_pTp, t * AH + (h - 1))
                        act.activation(p[h % 2][:], s[h % 2][:], ACT.Exp, bias=nmx[:, h:h + 1],
                                       accum_out=rs[:, h:h + 1]).then_inc(s_p, 1)
                        act.wait_ge(s_pTp, t * AH + (h + 1))
                        if not (first and h < 2):
                            act.wait_ge(s_pv, t * AH + (h - 1))
                        act.activation(pT[h % 2][:], tP[h % 2][:], ACT.Copy).then_inc(s_pT, 1)
                        if h in (0, 4, 5):
                            next(work, None)
                        if h == 5:
                            act.wait_ge(s_hm, t + 1)
                            act.activation(hr[:], hr[:], ACT.Sqrt).then_inc(s_hrt, 1)
                    act.wait_ge(s_dif, t + 1)
                    act.activation(es[:], es[:], ACT.Exp).then_inc(s_es, 1)

                def tail(t, cnd):
                    first = isinstance(t, int) and t == 0
                    act.wait_ge(s_mT, t + 1)
                    act.activation(mixT[:, 4:8, :].rearrange("p k n -> p (k n)"), uP[1][:], ACT.Copy).then_inc(s_mTa, 1)
                    yield
                    act.wait_ge(s_x1, t * 2 + 2)
                    if not first:
                        act.wait_ge(s_h2o, t * 32)
                    act.activation(xn[:], x1[:], ACT.Square, accum_out=ss[:]).then_inc(s_sq, 1)
                    yield
                    act.wait_ge(s_ms, t + 1)
                    act.activation(ss[:], ss[:], ACT.Sqrt).then_inc(s_rt, 1)
                    yield
                    act.wait_ge(s_xT, t + 1)
                    for k in range(4, KD):
                        last = act.activation(h2T[:, k, :], uP[2][:, (k - 4) * P:(k - 3) * P], ACT.Identity,
                                              bias=g.shift[:, 1, k, cnd:cnd + 1], scale=g.scale[:, 1, k, cnd:cnd + 1])
                    last.then_inc(s_hTa, 1)
                    act.wait_ge(s_hTa, t + 1)
                    act.wait_ge(s_hTd, t + 1)
                    act.dma_start(g.h2T_dram[t], h2T[:].rearrange("p k n -> p (k n)")).then_inc(s_h2o, 16)
                    act.wait_ge(s_h2p, t + 1)
                    act.activation(h2[:, 512:D], uP[1][:], ACT.Copy).then_inc(s_h2a, 1)
                    act.wait_ge(s_h2a, t + 1)
                    act.wait_ge(s_h2d, t + 1)
                    act.dma_start(g.h2_dram[t], h2[:]).then_inc(s_h2o, 16)

                run(act, front, tail)
                act.wait_ge(s_h2o, TILES * 32)

            @block.vector
            def _(dve):
                def front(t, work):
                    first = isinstance(t, int) and t == 0
                    c = Count(dve, s_front, FRONT, t)
                    dve.wait_ge(s_hs, t + 1)
                    c.link(dve.tensor_reduce(hr[:], hq[:].rearrange("p (h n) -> p h n", h=MH), AX.X, ALU.add))
                    dve.tensor_scalar(hr[:], hr[:], 1.0 / P, EPS, ALU.mult, ALU.add).then_inc(s_hm, 1)
                    dve.wait_ge(s_q, t * 32 + 32)
                    for h in range(AH):
                        dve.wait_ge(s_sc, t * AH + (h + 1))
                        if not (first and h < 2):
                            dve.wait_ge(s_p, t * AH + (h - 1))
                        dve.sem_inc(g.s_tick, 1)
                        dve.tensor_tensor_reduce(out=s[h % 2][:], in0=sP[h % 2][:], in1=mask[:], scale=float(ADH) ** -0.5,
                                                 scalar=sink[:, h:h + 1], op0=ALU.add, op1=ALU.max,
                                                 accum_out=mxs[:, h:h + 1]).then_inc(s_s, 1)
                        dve.wait_ge(s_s, t * AH + (h + 1))
                        dve.tensor_scalar(nmx[:, h:h + 1], mxs[:, h:h + 1], -1.0, None, ALU.mult).then_inc(s_nm, 1)
                        if h == 1:
                            dve.wait_ge(s_sge, t + 1)
                            c.link(dve.tensor_scalar(sg[:], sg[:], 1.0, None, ALU.add))
                            c.link(dve.reciprocal(sg[:], sg[:]))
                        if h in (0, 3, 5, 6):
                            next(work, None)
                    dve.wait_ge(s_nm, t * AH + AH)
                    if not first:
                        dve.wait_ge(s_mixa, t)
                    dve.tensor_tensor(es[:], sink[:], nmx[:], ALU.add).then_inc(s_dif, 1)
                    dve.wait_ge(s_hrt, t + 1)
                    dve.reciprocal(hr[:], hr[:]).then_inc(s_hr, 1)
                    next(work, None)
                    dve.wait_ge(s_es, t + 1)
                    dve.wait_ge(s_p, t * AH + AH)
                    c.link(dve.tensor_tensor(es[:], es[:], rs[:], ALU.add))
                    c.link(dve.reciprocal(es[:], es[:]))
                    dve.wait_ge(s_pv, t * AH + AH)
                    if not first:
                        dve.wait_ge(s_mT, t)
                    dve.tensor_tensor(mix[:, MW:D].rearrange("p (h n) -> p h n", h=AH),
                                      aP[:].rearrange("p (h n) -> p h n", h=AH),
                                      es[:].unsqueeze(2).to_broadcast([P, AH, ADH]), ALU.mult).then_inc(s_mixa, 1)

                def tail(t, cnd):
                    first = isinstance(t, int) and t == 0
                    c = Count(dve, s_tail, TAIL, t)
                    dve.wait_ge(s_mT, t + 1)
                    dve.tensor_copy(mixT[:, 0:4, :].rearrange("p k n -> p (k n)"), uP[0][:]).then_inc(s_mTd, 1)
                    yield
                    dve.wait_ge(s_x, t * 16 + 16)
                    if not first:
                        dve.wait_ge(s_x1o, t * 16)
                    for half in range(2):
                        hc = slice(half * 512, (half + 1) * 512)
                        dve.wait_ge(s_wo_mm, t * 2 + (half + 1))
                        c.link(dve.tensor_tensor(x1[:, hc], uP[2 - 2 * half][:], g.gate1[:, cnd, hc], ALU.mult))
                        dve.tensor_tensor(x1[:, hc], x1[:, hc], x[:, hc], ALU.add).then_inc(s_x1, 1)
                    yield
                    dve.wait_ge(s_sq, t + 1)
                    dve.tensor_scalar(ss[:], ss[:], 1.0 / D, EPS, ALU.mult, ALU.add).then_inc(s_ms, 1)
                    yield
                    dve.wait_ge(s_rt, t + 1)
                    c.link(dve.reciprocal(ss[:], ss[:]))
                    dve.tensor_scalar(xn[:], x1[:], ss[:], None, ALU.mult).then_inc(s_xn, 1)
                    yield
                    dve.wait_ge(s_xT, t + 1)
                    if not first:
                        dve.wait_ge(s_h2o, t * 32)
                    for k in range(4):
                        last = dve.tensor_scalar(h2T[:, k, :], uP[1][:, k * P:(k + 1) * P], g.scale[:, 1, k, cnd:cnd + 1],
                                                 g.shift[:, 1, k, cnd:cnd + 1], ALU.mult, ALU.add)
                    last.then_inc(s_hTd, 1)
                    yield
                    dve.wait_ge(s_h2p, t + 1)
                    dve.tensor_copy(h2[:, 0:512], uP[0][:]).then_inc(s_h2d, 1)

                dve.wait_ge(s_small, 64)
                run(dve, front, tail)


def peer(nc, g, io):
    PAIR = 2 * GROUP
    TURNS = SLOTS // PAIR
    NG = NSIDE // 4
    LINKS = NG * 4 + 1 + 2 * 4 + 13
    BATCH = 2
    NB = PAIR // BATCH
    LOW = -3.0e38
    with ExitStack() as ctx:
        def sb(name, shape, dt=F32):
            return ctx.enter_context(nc.sbuf_tensor(name, shape, dt))

        def sem(name):
            return ctx.enter_context(nc.semaphore(name))

        w_q = sb("pe_w_q", [P, KD, 2 * D])
        subT = sb("pe_subT", [P, 2, P])
        h2T = sb("pe_h2T", [P, KD, P])
        qT = [sb(f"pe_qT{i}", [P, 4, P]) for i in range(2)]
        sc = sb("pe_scores", [P, NSIDE, P])
        rest = sb("pe_rest", [P, NSIDE, P])
        val = sb("pe_val", [P, NSIDE, TOPK])
        idx = sb("pe_idx", [P, NSIDE, TOPK], U32)
        idf = sb("pe_idf", [P, NSIDE, TOPK])
        cand = sb("pe_cand", [P, PH, TOPK * TOPK])
        crest = rest[:].rearrange("p (h s) k -> p h (s k)", s=2)
        top = sb("pe_top", [P, PH, TOPK])
        pos = sb("pe_pos", [P, PH, TOPK], U32)
        psel = sb("pe_pos_part", [P, 2, SLOTS], U32)
        pself = sb("pe_pos_partf", [P, 2, SLOTS])
        iota = sb("pe_iota", [P, TOPK])
        ab = sb("pe_ab", [P, 2, SLOTS])
        gsum = sb("pe_gsum", [P, PH])
        gex = sb("pe_gexp", [P, PH, TOPK])
        qP = [ctx.enter_context(nc.psum_tensor(f"pe_qP{i}", [P, 4, P], F32)) for i in range(2)]
        cP = [ctx.enter_context(nc.psum_tensor(f"pe_cP{i}", [P, 4, P], F32)) for i in range(2)]
        ring = [sb(f"pe_ring{i}", [P, 2 * D]) for i in range(GROUP)]
        idg = [sb(f"pe_fetch_idx{i}", [P, GROUP], U32) for i in range(2)]
        h2 = sb("pe_h2", [P, D])
        x1 = sb("pe_x1", [P, D])
        gated = sb("pe_gated_sum", [P, D])
        dot = sb("pe_dot", [P, PAIR])
        gelu = sb("pe_gelu", [P, PAIR])
        w = sb("pe_w", [P, PAIR])
        diag = sb("pe_diag", [P, GROUP, P])
        zero = sb("pe_zero", [P, 512])
        acc = [ctx.enter_context(nc.psum_tensor(f"pe_acc{i}", [P, 512], F32)) for i in range(2)]

        s_small = sem("pe_small_in")
        s_const = sem("pe_const_ready")
        s_wq = sem("pe_w_q_in")
        s_hT = sem("pe_h2T_in")
        s_q = sem("pe_q_done")
        s_qT = sem("pe_qT_ready")
        s_c = sem("pe_scores_done")
        s_sc = sem("pe_scores_ready")
        s_top = sem("pe_sides_done")
        s_mid = sem("pe_dve_chain")
        s_gd = sem("pe_gate_diff")
        s_ge = sem("pe_gate_exp")
        s_route = sem("pe_route_done")
        s_g = [sem(f"pe_fetched{i}") for i in range(GROUP)]
        s_idx = sem("pe_fetch_idx_ready")
        s_h = sem("pe_h2_in")
        s_x = sem("pe_x1_in")
        s_dot = sem("pe_dot_ready")
        s_gelu = sem("pe_gelu_ready")
        s_w = sem("pe_w_ready")
        s_diag = sem("pe_diag_ready")
        s_pv = sem("pe_slot_done")
        s_acc = sem("pe_acc_done")
        s_gated = sem("pe_gated")
        s_out = sem("pe_out_ready")
        s_st = sem("pe_stored")

        with nc.Block() as block:
            @block.sync
            def _(sp):
                flat = h2T[:].rearrange("p k n -> p (k n)")
                sp.dma_start(subT[:], io.subT).then_inc(s_small, 16)
                sp.dma_start(flat, g.h2T_dram[0]).then_inc(s_hT, 16)
                for k in range(KD):
                    sp.dma_start(w_q[:, k, :], io.w_q[k * P:(k + 1) * P, :]).then_inc(s_wq, 16)
                sp.dma_start(h2[:], g.h2_dram[0]).then_inc(s_h, 16)
                sp.dma_start(x1[:], g.x1_dram[0]).then_inc(s_x, 16)

                def after(t, more=True):
                    sp.wait_ge(s_dot, t * SLOTS + SLOTS)
                    sp.dma_start(h2[:], g.h2_dram[t + 1]).then_inc(s_h, 16)
                    sp.wait_ge(s_out, t + 1)
                    sp.dma_start(io.y[t], x1[:]).then_inc(s_st, 16)
                    sp.wait_ge(s_st, t * 16 + 16)
                    sp.dma_start(x1[:], g.x1_dram[t + 1]).then_inc(s_x, 16)

                sp.wait_ge(s_q, NG)
                sp.dma_start(flat, g.h2T_dram[1]).then_inc(s_hT, 16)
                with sp.Fori(0, TILES - 2) as t:
                    sp.wait_ge(s_q, t * NG + 2 * NG)
                    sp.dma_start(flat, g.h2T_dram[t + 2]).then_inc(s_hT, 16)
                    after(t)
                after(TILES - 2)
                sp.wait_ge(s_out, TILES)
                sp.dma_start(io.y[TILES - 1], x1[:]).then_inc(s_st, 16)
                sp.wait_ge(s_st, TILES * 16)

            @block.gpsimd
            def _(pool):
                pool.iota(iota[:], pattern=[[1, TOPK]], base=0, channel_multiplier=0,
                          allow_small_or_imprecise_dtypes=True).then_inc(s_const, 1)
                pool.memset(zero[:], 0.0).then_inc(s_const, 1)

                def turn(t, r, first=False):
                    n = t * TURNS + r
                    for half in range(2):
                        if not first:
                            pool.wait_ge(s_dot, n * PAIR - PAIR + GROUP * (half + 1))
                            pool.sem_inc(g.s_tick, 1)
                        pool.tensor_copy(idg[half][:], g.eidx[:, t, bass.ds(r * PAIR + half * GROUP, GROUP)]).then_inc(s_idx, 1)
                        pool.wait_ge(s_idx, n * 2 + (half + 1))
                        for j in range(GROUP):
                            i = half * GROUP + j
                            if not (first and half == 0):
                                pool.wait_ge(s_pv, n * PAIR + (i - GROUP + 1))
                            pool.sem_inc(g.s_tick, 1)
                            pool.indirect_dma_start(out=ring[j][:], out_offset=None, in_=io.uv,
                                                    in_offset=bass.IndirectOffsetOnAxis(ap=idg[half][:, j:j + 1], axis=0),
                                                    ).then_inc(s_g[j], 16)

                pool.wait_ge(s_route, 1)
                turn(0, 0, True)
                with pool.Fori(1, TURNS) as r:
                    turn(0, r)
                with pool.Fori(1, TILES) as t:
                    pool.wait_ge(s_route, t + 1)
                    pool.sem_inc(g.s_tick, 1)
                    with pool.Fori(0, TURNS) as r:
                        turn(t, r)

            @block.tensor
            def _(pe):
                def query(t, b, j, first=False):
                    if j == 0 and not (first and b < 2):
                        pe.wait_ge(s_qT, t * NG + (b - 1))
                    if j == 0 and b == 0:
                        pe.wait_ge(s_hT, t * 16 + 16)
                    i = 4 * b + j
                    for k in range(KD):
                        mm = pe.matmul(qP[b % 2][:, j, :], w_q[:, k, i * P:(i + 1) * P], h2T[:, k, :],
                                       start=(k == 0), stop=(k == KD - 1))
                    if j == 3:
                        mm.then_inc(s_q, 1)

                def scores(t, b, first=False):
                    pe.wait_ge(s_qT, t * NG + (b + 1))
                    if not (first and b < 2):
                        pe.wait_ge(s_sc, t * NG + (b - 1))
                    for j in range(4):
                        mm = pe.matmul(cP[b % 2][:, j, :], qT[b % 2][:, j, :], subT[:, j % 2, :], start=True, stop=True)
                    mm.then_inc(s_c, 1)

                def turn(t, r, retrieve=False):
                    n = t * TURNS + r
                    for i in range(PAIR):
                        pe.wait_ge(s_diag, n * PAIR + (i + 1))
                        for b in range(2):
                            mm = pe.matmul(acc[b][:], diag[:, i % GROUP, :], ring[i % GROUP][:, D + b * 512:D + (b + 1) * 512],
                                           start=False, stop=False)
                        mm.then_inc(s_pv, 1)
                        m = r * NB + i // BATCH if retrieve else 0
                        if retrieve and i % BATCH == 1:
                            if m < NSIDE:
                                query(t + 1, m // 4, m % 4)
                            if m >= 7 and (m - 7) % 4 == 0 and (m - 7) // 4 < NG:
                                scores(t + 1, (m - 7) // 4)

                def tile(t, first=False, more=True):
                    if not first:
                        pe.wait_ge(s_gated, t * 2)
                    for b in range(2):
                        pe.matmul(acc[b][:], zero[:, 0:P], zero[:], start=True, stop=False)
                    if more:
                        for r in range(3):
                            turn(t, r, True)
                    with pe.Fori(3 if more else 0, TURNS) as r:
                        turn(t, r)
                    for b in range(2):
                        mm = pe.matmul(acc[b][:], zero[:, 0:P], zero[:], start=False, stop=True)
                    mm.then_inc(s_acc, 1)

                pe.wait_ge(s_const, 2)
                pe.wait_ge(s_small, 16)
                pe.wait_ge(s_wq, 16 * KD)
                for b in range(NG):
                    for j in range(4):
                        query(0, b, j, True)
                    if b >= 1:
                        scores(0, b - 1, True)
                scores(0, NG - 1, True)
                tile(0, True)
                with pe.Fori(1, TILES - 1) as t:
                    tile(t)
                tile(TILES - 1, more=False)

            @block.scalar
            def _(act):
                def turned(t, b, first=False):
                    act.wait_ge(s_q, t * NG + (b + 1))
                    if not (first and b < 2):
                        act.wait_ge(s_c, t * NG + (b - 1))
                    act.activation(qT[b % 2][:], qP[b % 2][:], ACT.Copy).then_inc(s_qT, 1)

                def out(t, b, first=False):
                    act.wait_ge(s_c, t * NG + (b + 1))
                    if not first:
                        act.wait_ge(s_top, t * NG + (b + 1 - NG))
                    act.activation(sc[:, 4 * b:4 * b + 4, :], cP[b % 2][:], ACT.Copy).then_inc(s_sc, 1)

                def gate_exp(t):
                    act.wait_ge(s_gd, t + 1)
                    act.activation(gex[:], gex[:], ACT.Exp).then_inc(s_ge, 1)

                def turn(t, r, first=False, retrieve=False):
                    n = t * TURNS + r
                    for q in range(NB):
                        sl = slice(q * BATCH, (q + 1) * BATCH)
                        act.wait_ge(s_dot, n * PAIR + BATCH * (q + 1))
                        act.activation(gelu[:, sl], dot[:, sl], ACT.Gelu_apprx_tanh).then_inc(s_gelu, 1)
                        act.wait_ge(s_w, n * NB + (q + 1))
                        for i in range(q * BATCH, (q + 1) * BATCH):
                            if not (first and i < GROUP):
                                act.wait_ge(s_pv, n * PAIR + (i - GROUP + 1))
                            act.activation(diag[:, i % GROUP, :], g.ident[:], ACT.Copy, scale=w[:, i:i + 1]).then_inc(s_diag, 1)
                        m = r * NB + q if retrieve else 0
                        if retrieve:
                            if m >= 6 and (m - 6) % 4 == 0 and (m - 6) // 4 < NG:
                                turned(t + 1, (m - 6) // 4)
                            if m >= 10 and (m - 10) % 4 == 0 and (m - 10) // 4 < NG:
                                out(t + 1, (m - 10) // 4)

                def tile(t, first=False, more=True):
                    if first or more:
                        for r in range(3):
                            turn(t, r, first and r == 0, more)
                        with act.Fori(3, 5) as r:
                            turn(t, r)
                        gate_exp(t + 1)
                        with act.Fori(5, TURNS) as r:
                            turn(t, r)
                    else:
                        with act.Fori(0, TURNS) as r:
                            turn(t, r)

                for b in range(NG):
                    turned(0, b, True)
                    if b >= 1:
                        out(0, b - 1, True)
                out(0, NG - 1, True)
                gate_exp(0)
                tile(0, True)
                with act.Fori(1, TILES - 1) as t:
                    tile(t)
                tile(TILES - 1, more=False)

            @block.vector
            def _(dve):
                def top16(c, rows, src, left, v, ix, last_sem=None):
                    end = rows[-1]
                    for r in rows[:-1]:
                        dve.max(v[:, r, 0:8], src[:, r, :])
                    c.link(dve.max(v[:, end, 0:8], src[:, end, :]))
                    yield
                    for r in rows[:-1]:
                        dve.match_replace(left[:, r, :], v[:, r, 0:8], src[:, r, :], LOW)
                    c.link(dve.match_replace(left[:, end, :], v[:, end, 0:8], src[:, end, :], LOW))
                    yield
                    for r in rows[:-1]:
                        dve.max(v[:, r, 8:16], left[:, r, :])
                    c.link(dve.max(v[:, end, 8:16], left[:, end, :]))
                    for r in rows[:2]:
                        dve.max_index(ix[:, r, 0:8], v[:, r, 0:8], src[:, r, :])
                    yield
                    for r in rows[2:]:
                        ins = dve.max_index(ix[:, r, 0:8], v[:, r, 0:8], src[:, r, :])
                        if last_sem is not None and r == end:
                            ins.then_inc(last_sem, 1)
                    for r in rows[:-1]:
                        dve.max_index(ix[:, r, 8:16], v[:, r, 8:16], left[:, r, :])
                    c.link(dve.max_index(ix[:, end, 8:16], v[:, end, 8:16], left[:, end, :]))
                    yield

                def retrieval(c, t):
                    for b in range(NG):
                        dve.wait_ge(s_sc, t * NG + (b + 1))
                        dve.sem_inc(g.s_tick, 1)
                        yield from top16(c, range(4 * b, 4 * b + 4), sc, rest, val, idx, s_top)
                    v4 = val[:].rearrange("p (h s) k -> p h s k", s=2)
                    c4 = cand[:].rearrange("p h (a b) -> p h a b", a=TOPK)
                    c.link(dve.tensor_tensor(c4, v4[:, :, 0, :].unsqueeze(3).to_broadcast([P, PH, TOPK, TOPK]),
                                             v4[:, :, 1, :].unsqueeze(2).to_broadcast([P, PH, TOPK, TOPK]), ALU.add))
                    yield
                    for b in range(2):
                        yield from top16(c, range(4 * b, 4 * b + 4), cand, crest, top, pos)
                    dve.tensor_tensor(gex[:], top[:], top[:, :, 0:1].to_broadcast([P, PH, TOPK]),
                                      ALU.subtract).then_inc(s_gd, 1)
                    posf = pos[:].rearrange("p h k -> p (h k)")
                    c.link(dve.tensor_scalar(psel[:, 0, :], posf, 4, None, ALU.logical_shift_right))
                    c.link(dve.tensor_scalar(psel[:, 1, :], posf, TOPK - 1, None, ALU.bitwise_and))
                    c.link(dve.tensor_copy(pself[:], psel[:]))
                    c.link(dve.tensor_copy(idf[:], idx[:]))
                    yield
                    i4 = idf[:].rearrange("p (h s) k -> p h s k", s=2)
                    for side, hit in enumerate((cand[:], crest)):
                        h3 = hit.rearrange("p h (a b) -> p (h a) b", a=TOPK)
                        h4 = hit.rearrange("p h (a b) -> p h a b", a=TOPK)
                        c.link(dve.tensor_tensor(h3, pself[:, side, :].unsqueeze(2).to_broadcast([P, SLOTS, TOPK]),
                                                 iota[:].unsqueeze(1).to_broadcast([P, SLOTS, TOPK]), ALU.is_equal))
                        yield
                        c.link(dve.tensor_tensor(h4, h4, i4[:, :, side, :].unsqueeze(2).to_broadcast([P, PH, TOPK, TOPK]),
                                                 ALU.mult))
                        yield
                        c.link(dve.tensor_reduce(ab[:, side, :], h3, AX.X, ALU.add))
                        yield
                    c.link(dve.scalar_tensor_tensor(g.eidx[:, t, :], ab[:, 0, :], float(P), ab[:, 1, :], ALU.mult, ALU.add))
                    dve.wait_ge(s_ge, t + 1)
                    c.link(dve.tensor_reduce(gsum[:], gex[:], AX.X, ALU.add))
                    c.link(dve.reciprocal(gsum[:], gsum[:]))
                    dve.tensor_tensor(g.gates[:, t, :].rearrange("p (h k) -> p h k", h=PH), gex[:],
                                      gsum[:].unsqueeze(2).to_broadcast([P, PH, TOPK]), ALU.mult).then_inc(s_route, 1)
                    dve.wait_ge(s_route, t + 1)
                    dve.sem_inc(g.s_tick, 1)
                    assert c.k == LINKS, c.k

                idle = iter(())

                def turn(t, r, work):
                    n = t * TURNS + r
                    for q in range(NB):
                        sl = slice(q * BATCH, (q + 1) * BATCH)
                        for i in range(q * BATCH, (q + 1) * BATCH):
                            j = i % GROUP
                            dve.wait_ge(s_g[j], n * 32 + 16 * (i // GROUP + 1))
                            dve.tensor_tensor_reduce(out=ring[j][:, 0:D], in0=ring[j][:, 0:D], in1=h2[:],
                                                     scale=1.0, scalar=0.0, op0=ALU.mult, op1=ALU.add,
                                                     accum_out=dot[:, i:i + 1]).then_inc(s_dot, 1)
                        next(work, None)
                        dve.wait_ge(s_gelu, n * NB + (q + 1))
                        dve.tensor_tensor(w[:, sl], gelu[:, sl], g.gates[:, t, bass.ds(r * PAIR + q * BATCH, BATCH)],
                                          ALU.mult).then_inc(s_w, 1)

                def tile(t, cnd, more=True):
                    dve.wait_ge(s_h, t * 16 + 16)
                    dve.sem_inc(g.s_tick, 1)
                    if more:
                        work = retrieval(Count(dve, s_mid, LINKS, t + 1, g.s_tick), t + 1)
                        turn(t, 0, idle)
                        turn(t, 1, chain(repeat(None, 4), work))
                        for r in range(2, TURNS):
                            turn(t, r, work)
                    else:
                        with dve.Fori(0, TURNS) as r:
                            turn(t, r, idle)
                    dve.wait_ge(s_acc, t + 1)
                    dve.wait_ge(s_x, t * 16 + 16)
                    for b in range(2):
                        hc = slice(b * 512, (b + 1) * 512)
                        dve.tensor_tensor(gated[:, hc], acc[b][:], g.gate2[:, cnd, hc], ALU.mult).then_inc(s_gated, 1)
                    dve.wait_ge(s_gated, t * 2 + 2)
                    dve.tensor_tensor(x1[:], x1[:], gated[:], ALU.add).then_inc(s_out, 1)

                dve.wait_ge(s_const, 2)
                c = Count(dve, s_mid, LINKS, 0, g.s_tick)
                for _ in retrieval(c, 0):
                    pass
                tile(0, 0)
                with dve.Fori(1, TILES - 1) as t:
                    tile(t, 1)
                tile(TILES - 1, 1, more=False)


def program(nc, tensors):
    ctx = ExitStack()
    io = Names()
    io.x = tensors["x"]
    io.cond_cols = tensors["cond_cols"]
    io.w_ada = tensors["w_ada"]
    io.b_ada = tensors["b_ada"]
    io.norm_cols = tensors["norm_cols"]
    io.w_in = tensors["w_in"]
    io.b_gates = tensors["b_gates"]
    io.head_norm = tensors["head_norm"]
    io.trig = tensors["trig"]
    io.m0 = tensors["m0"]
    io.c0 = tensors["c0"]
    io.cache_kT = tensors["cache_kT"]
    io.cache_v = tensors["cache_v"]
    io.att_mask = tensors["att_mask"]
    io.sink = tensors["sink"]
    io.mh_g = tensors["mh_g"]
    io.w_out = tensors["w_out"]
    io.w_q = tensors["w_q"]
    io.subT = tensors["subT"]
    io.uv = tensors["uv"]
    io.y = tensors["y"]
    io.new_kv = tensors["new_kv"]
    io.new_c = tensors["new_c"]
    io.new_m = tensors["new_m"]
    with ctx:
        def sb(name, shape, dt=F32):
            return ctx.enter_context(nc.sbuf_tensor(name, shape, dt))

        def dram(name, shape):
            return nc.dram_tensor(name, shape, F32, kind="Internal").ap()

        g = Names()
        g.ident = sb("ident", [P, P])
        g.sel = sb("sel", [MH, MH, P])
        g.rstd = sb("rstd", [P, TILES])
        g.shift = sb("shift", [P, 2, KD, COND])
        g.scale = sb("scale", [P, 2, KD, COND])
        g.gate2 = sb("gate2", [P, COND, D])
        g.new_kv = sb("new_kv", [P, 2 * AKV * ADH])
        g.eidx = sb("eidx", [P, TILES, SLOTS], U32)
        g.gates = sb("gates", [P, TILES, SLOTS])
        g.s_w_in = ctx.enter_context(nc.semaphore("w_in_in"))
        g.s_tick = ctx.enter_context(nc.semaphore("tick"))
        g.s_new_kv = ctx.enter_context(nc.semaphore("new_kv_ready"))
        g.kv_dram = dram("kv_scratch", (TILES, P, 2 * MW))
        g.qkT_dram = dram("qkT_scratch", (TILES, P, 2 * MW))
        g.aqT_dram = dram("aqT_scratch", (TILES, P, 512))
        g.x1_dram = dram("x1_scratch", (TILES, P, D))
        g.h2_dram = dram("h2_scratch", (TILES, P, D))
        g.h2T_dram = dram("h2T_scratch", (TILES, P, D))
        with ExitStack() as mixers:
            def msb(name, shape, dt=F32):
                return mixers.enter_context(nc.sbuf_tensor(name, shape, dt))

            g.gate1 = msb("gate1", [P, COND, D])
            g.neg_after = msb("neg_after", [P, MH, P])
            g.neg_before = msb("neg_before", [P, MH, P])
            with ExitStack() as weights:
                g.w_in = weights.enter_context(nc.sbuf_tensor("w_in", [P, KD, IN_COLS], F32, side="right"))
                conditioning(nc, g, io)
                g.mo = msb("mlstm_o", [P, TILES, MW])
                g.akT = msb("att_kT", [P, AKV, (TILES + 2) * P])
                g.av = msb("att_v", [P, TILES + 2, AKV * ADH])
                g.grow = [msb(f"gate_rows{i}", [MH, TILES * P]) for i in range(4)]
                project_in(nc, g, io)
            g.h_dir = [msb(f"h_dir{i}", [P, TILES, MW]) for i in range(2)]
            mlstm(nc, g, io)
            attend(nc, g, io)
        peer(nc, g, io)


def layout(inputs):
    A = {k: np.asarray(v) for k, v in inputs.items()}

    def spread(a, n=P):
        return np.broadcast_to(a, (n,) + a.shape)

    def cols(a):
        return a.reshape(a.shape[0], KD, P).transpose(2, 0, 1)

    GRID_W = 64
    T = (TILES - 1) * P
    quarter = ADH // 4
    inv = (np.float32(10000.0) ** (-np.arange(quarter, dtype=np.float32) / np.float32(quarter))).astype(np.float32)
    tok = np.arange(T)
    cos, sin = [], []
    for pos in (tok // GRID_W, tok % GRID_W):
        ang = pos.astype(np.float32)[:, None] * inv[None, :]
        cos += [np.cos(ang)] * 2
        sin += [-np.sin(ang), np.sin(ang)]
    trig = np.zeros((TILES * P, 2 * ADH), np.float32)
    trig[:P, :ADH] = 1.0
    trig[P:, :ADH] = np.concatenate(cos, 1)
    trig[P:, ADH:] = np.concatenate(sin, 1)
    mask = np.full((TILES, P, 4 * P), NEG, np.float32)
    mask[0, :, 2 * P:3 * P] = 0.0
    q = np.arange(P)[:, None]
    for t in range(1, TILES):
        kpos = (t - 2) * P + np.arange(3 * P)[None, :]
        ok = (kpos >= 0) & (kpos < T) & (np.abs(kpos - ((t - 1) * P + q)) <= P)
        mask[t, :, :P] = 0.0
        mask[t, :, P:][ok] = 0.0
    w = A["w_in"][0]
    edges = [0, 512, 1024, 1536, 2048, 2064, 2576, 2704, 2832]
    wq, wk, wv, wo, wg, waq, wak, wav = (w[:, a:b] for a, b in zip(edges[:-1], edges[1:]))
    ck = A["cache_attn_k"][0, 0].transpose(1, 2, 0)
    return {
        "x": np.concatenate([A["x_prompt"][0], A["x_sample"][0]]).reshape(TILES, P, D),
        "cond_cols": np.stack([A["c_ctx"], A["c"][0]]).reshape(COND, KD, P).transpose(2, 1, 0),
        "w_ada": A["w_ada"][0],
        "b_ada": spread(A["b_ada"][0], COND),
        "norm_cols": cols(np.stack([A["norm1_g"][0], A["norm2_g"][0]])),
        "w_in": np.concatenate([wq, wk, wv, wo, waq, wak, wav, wg], axis=1),
        "b_gates": spread(A["b_gates"][0]),
        "head_norm": spread(np.concatenate([np.tile(A["q_norm_g"][0], AH), np.tile(A["k_norm_g"][0], AKV)])),
        "trig": trig.reshape(TILES, P, 2 * ADH),
        "m0": A["state_mlstm_m"][0, 0].T,
        "c0": np.concatenate([A["state_mlstm_C"][0, 0], A["state_mlstm_n"][0, 0][..., None]], axis=-1).transpose(0, 2, 1, 3),
        "cache_kT": np.concatenate([ck, ck], axis=1).transpose(1, 0, 2),
        "cache_v": A["cache_attn_v"][0, 0].reshape(P, AKV * ADH),
        "att_mask": mask,
        "sink": spread(A["sink_logits"][0]),
        "mh_g": spread(A["mh_norm_g"][0]),
        "w_out": A["w_out"][0],
        "w_q": A["peer_w_q"][0],
        "subT": np.stack([A["peer_sub_a"][0], A["peer_sub_b"][0]]).transpose(2, 0, 1),
        "uv": np.concatenate([A["peer_u"][0], A["peer_v"][0]], axis=1),
    }


OUTS = {
    "y": (TILES, P, D),
    "new_kv": (P, 2 * AKV * ADH),
    "new_c": (2, P, MH, C1),
    "new_m": (2, MH, 1),
}


def kernel(**inputs):
    import concourse.bacc as bacc
    from concourse.bass_utils import run_bass_kernel_spmd

    nc = bacc.Bacc("TRN2", target_bir_lowering=False, num_devices=1)
    arrays, tensors = {}, {}
    for name, a in layout(inputs).items():
        a = np.ascontiguousarray(a)
        arrays[f"arg_{name}"] = a
        tensors[name] = nc.dram_tensor(f"arg_{name}", a.shape, mybir.dt.from_np(a.dtype), kind="ExternalInput").ap()
    for name, shape in OUTS.items():
        tensors[name] = nc.dram_tensor(f"result_{name}", shape, F32, kind="ExternalOutput").ap()
    program(nc, tensors)
    r = run_bass_kernel_spmd(nc, [arrays], core_ids=[0]).results[0]
    y, kv, cn, m = (r[f"result_{name}"] for name in OUTS)
    half = AKV * ADH
    cn = cn.transpose(0, 2, 1, 3)[None, None]
    return (y[0][None], y[1:].reshape(1, (TILES - 1) * P, D),
            kv[:, :half].reshape(1, 1, P, AKV, ADH), kv[:, half:].reshape(1, 1, P, AKV, ADH),
            np.ascontiguousarray(cn[..., :P]), np.ascontiguousarray(cn[..., P]), m[..., 0].reshape(1, 1, 2, MH))
```
